# Optimizing a Trainium2 kernel written in Bass

```python
import jax, jax.numpy as jnp
from jax import lax
import numpy as np

D_MODEL = 1024
BATCH = 1
SEQ = 128
DEPTH = 1
DEC_BATCH = 1
DEC_SEQ = 512
PAST_LEN = 256

GRID_W = 64
N_HEADS = 8
KV_HEADS = 2
Q_PER_KV = N_HEADS // KV_HEADS
HEAD_DIM = 64
ATTN_WIDTH = N_HEADS * HEAD_DIM
KV_WIDTH = KV_HEADS * HEAD_DIM
Q_BLOCK = 128
ROPE_THETA = 10000.0
ROPE_PAIRS = HEAD_DIM // 4
R_HEADS = 8
R_HEAD_DIM = 64
R_WIDTH = R_HEADS * R_HEAD_DIM
DECAY_RANK = 64
ICLR_RANK = 64
GATE_RANK = 128
R_IN_WIDTH = 3 * R_WIDTH + DECAY_RANK + ICLR_RANK + GATE_RANK
IN_WIDTH = ATTN_WIDTH + 2 * KV_WIDTH + R_IN_WIDTH + 2 * D_MODEL
D_FF = 2816
N_MOD = 6
NORM_EPS = 1e-6
GN_EPS = 64e-5
DECAY_OFFSET = 0.5

kernel_name = "hybrid_dit_attn_rwkv7_prefix_step"

def _rmsnorm(x, g):
    xf = x.astype(jnp.float32)
    y = xf * lax.rsqrt(jnp.mean(xf * xf, axis=-1, keepdims=True) + NORM_EPS)
    return (y * g.astype(jnp.float32)).astype(x.dtype)

def _modulate(h, shift, scale):
    return h * (1 + scale[:, None, :]) + shift[:, None, :]

def _dwconv3(x, w):
    xp = jnp.pad(x, ((0, 0), (1, 1), (0, 0)))
    return xp[:, :-2] * w[0] + xp[:, 1:-1] * w[1] + xp[:, 2:] * w[2]

def _axial_rope_tables(rows):
    row = jnp.repeat(jnp.arange(rows), GRID_W).astype(jnp.float32)
    col = jnp.tile(jnp.arange(GRID_W), rows).astype(jnp.float32)
    inv = 1.0 / (ROPE_THETA ** (jnp.arange(ROPE_PAIRS, dtype=jnp.float32) / ROPE_PAIRS))
    ang = jnp.concatenate([row[:, None] * inv, col[:, None] * inv], axis=-1)
    return jnp.cos(ang), jnp.sin(ang)

def _apply_rope(x, cos, sin):
    x1, x2 = jnp.split(x, 2, axis=-1)
    cos = cos.astype(x.dtype)
    sin = sin.astype(x.dtype)
    return jnp.concatenate([x1 * cos - x2 * sin, x2 * cos + x1 * sin], axis=-1)

def _block_attention(q, k, v):
    b, h, t, d = q.shape
    nb = t // Q_BLOCK
    qb = jnp.moveaxis(q.reshape(b, KV_HEADS, Q_PER_KV, nb, Q_BLOCK, d), 3, 0)
    scale = d ** -0.5

    def one_block(qblk):
        s = jnp.einsum("bkgqd,bkld->bkgql", qblk, k).astype(jnp.float32) * scale
        p = jax.nn.softmax(s, axis=-1).astype(v.dtype)
        return jnp.einsum("bkgql,bkld->bkgqd", p, v)

    o = lax.map(one_block, qb)
    o = jnp.moveaxis(o, 0, 3).reshape(b, h, t, d)
    return o.transpose(0, 2, 1, 3).reshape(b, t, h * d)

def _wkv7_scan(r, w, k, v, kk, a, s0, reverse):
    def step(s, inp):
        r_t, w_t, k_t, v_t, kk_t, a_t = inp
        sa = jnp.einsum("bhvk,bhk->bhv", s, -kk_t)
        s = (s * w_t[:, :, None, :] + sa[..., None] * (kk_t * a_t)[:, :, None, :]
             + v_t[..., None] * k_t[:, :, None, :])
        return s, jnp.einsum("bhvk,bhk->bhv", s, r_t)

    xs = tuple(jnp.moveaxis(z, 1, 0) for z in (r, w, k, v, kk, a))
    s_final, ys = lax.scan(step, s0, xs, reverse=reverse)
    return jnp.moveaxis(ys, 0, 1), s_final

def _rwkv7_bidir(u, p, s0):
    b, t, _ = u.shape
    f32 = jnp.float32
    u = _dwconv3(u, p["rwkv_conv"])
    splits = np.cumsum([R_WIDTH, R_WIDTH, R_WIDTH, DECAY_RANK, ICLR_RANK]).tolist()
    r, k, v, wd, ad, gd = jnp.split(u, splits, axis=-1)

    def heads(z):
        return z.reshape(b, t, R_HEADS, R_HEAD_DIM).astype(f32)

    rh, kh, vh = heads(r), heads(k), heads(v)
    kk = heads(k * p["rwkv_k_k"])
    kk = kk * lax.rsqrt(jnp.sum(kk * kk, axis=-1, keepdims=True) + 1e-12)
    ka = p["rwkv_k_a"].reshape(R_HEADS, R_HEAD_DIM).astype(f32)
    r_k = p["rwkv_r_k"].astype(f32)
    wd_t = jnp.tanh(wd)
    ys, bonus, finals = [], [], []
    for d, reverse in enumerate((False, True)):
        logw = -jax.nn.softplus(-(p["rwkv_w0"][d] + wd_t @ p["rwkv_w2"][d])) - DECAY_OFFSET
        w = jnp.exp(-jnp.exp(heads(logw)))
        a = jax.nn.sigmoid(heads(p["rwkv_a0"][d] + ad @ p["rwkv_a2"][d]))
        kd = kh * (1 + (a - 1) * ka)
        y, s_fin = _wkv7_scan(rh, w, kd, vh, kk, a, s0[:, d].astype(f32), reverse)
        ys.append(y)
        bonus.append(jnp.sum(rh * kd * r_k, axis=-1, keepdims=True) * vh)
        finals.append(s_fin)
    y = ys[0] + ys[1]
    mu = jnp.mean(y, axis=-1, keepdims=True)
    var = jnp.mean(jnp.square(y - mu), axis=-1, keepdims=True)
    y = ((y - mu) * lax.rsqrt(var + GN_EPS)).reshape(b, t, R_WIDTH)
    y = (y * p["rwkv_ln_g"].astype(f32) + p["rwkv_ln_b"].astype(f32)
         + (bonus[0] + bonus[1]).reshape(b, t, R_WIDTH))
    g = jax.nn.sigmoid(gd) @ p["rwkv_g2"]
    return y.astype(u.dtype) * g, jnp.stack(finals, axis=1)

def _layer(x, mod, p, rope, ctx_k, ctx_v, s0):
    b, t, _ = x.shape
    shift1, scale1, gate1, shift2, scale2, gate2 = jnp.split(mod, N_MOD, axis=-1)
    h = _modulate(_rmsnorm(x, p["norm1_g"]), shift1, scale1)
    proj = h @ p["w_in"]
    splits = np.cumsum([ATTN_WIDTH, KV_WIDTH, KV_WIDTH, R_IN_WIDTH, D_MODEL]).tolist()
    q, k, v, u, ga, gr = jnp.split(proj, splits, axis=-1)
    q = _rmsnorm(q.reshape(b, t, N_HEADS, HEAD_DIM), p["q_norm_g"]).transpose(0, 2, 1, 3)
    k = _rmsnorm(k.reshape(b, t, KV_HEADS, HEAD_DIM), p["k_norm_g"]).transpose(0, 2, 1, 3)
    v = v.reshape(b, t, KV_HEADS, HEAD_DIM).transpose(0, 2, 1, 3)
    if rope is None:
        keys, vals = k, v
    else:
        cos, sin = rope
        q = _apply_rope(q, cos, sin)
        keys = jnp.concatenate([_apply_rope(k, cos, sin), ctx_k.astype(k.dtype)], axis=2)
        vals = jnp.concatenate([v, ctx_v.astype(v.dtype)], axis=2)
    attn_o = _block_attention(q, keys, vals)
    rwkv_o, s_final = _rwkv7_bidir(u, p, s0)
    merged = (jax.nn.sigmoid(ga) * (attn_o @ p["w_attn_br"])
              + jax.nn.sigmoid(gr) * (rwkv_o @ p["w_rwkv_br"]))
    x = x + gate1[:, None, :] * (merged @ p["w_out"])
    h2 = _modulate(_rmsnorm(x, p["norm2_g"]), shift2, scale2)
    up = _dwconv3(h2 @ p["ffn_up"], p["ffn_conv"])
    up_u, up_g = jnp.split(up, 2, axis=-1)
    x = x + gate2[:, None, :] * ((jax.nn.silu(up_g) * up_u) @ p["ffn_down"])
    return x, k, v, s_final

def setup_inputs(seed: int = 0) -> dict:
    key = jax.random.key(seed)
    ks = jax.random.split(key, 40)
    nrm = jax.random.normal
    f32 = jnp.float32
    L = DEPTH
    conv_base = jnp.array([0.3, 1.0, 0.3], dtype=f32)[:, None]
    return {
        "x_prompt": nrm(ks[0], (BATCH, SEQ, D_MODEL), f32),
        "x_sample": nrm(ks[1], (DEC_BATCH, DEC_SEQ, D_MODEL), f32),
        "cache_k": nrm(ks[2], (DEC_BATCH, L, KV_HEADS, PAST_LEN, HEAD_DIM), f32),
        "cache_v": nrm(ks[3], (DEC_BATCH, L, KV_HEADS, PAST_LEN, HEAD_DIM), f32),
        "state_rwkv": 0.5 * nrm(ks[4], (DEC_BATCH, L, 2, R_HEADS, R_HEAD_DIM, R_HEAD_DIM), f32),
        "c": nrm(ks[5], (DEC_BATCH, D_MODEL), f32),
        "c_ctx": nrm(ks[6], (D_MODEL,), f32),
        "w_ada": 0.5 * D_MODEL ** -0.5 * nrm(ks[7], (L, D_MODEL, N_MOD * D_MODEL), f32),
        "b_ada": 0.02 * nrm(ks[8], (L, N_MOD * D_MODEL), f32),
        "norm1_g": 1.0 + 0.02 * nrm(ks[9], (L, D_MODEL), f32),
        "w_in": D_MODEL ** -0.5 * nrm(ks[10], (L, D_MODEL, IN_WIDTH), f32),
        "q_norm_g": 1.0 + 0.02 * nrm(ks[11], (L, HEAD_DIM), f32),
        "k_norm_g": 1.0 + 0.02 * nrm(ks[12], (L, HEAD_DIM), f32),
        "rwkv_conv": conv_base + 0.1 * nrm(ks[13], (L, 3, R_IN_WIDTH), f32),
        "rwkv_w0": 1.5 * nrm(ks[14], (L, 2, R_WIDTH), f32) - 1.5,
        "rwkv_w2": 0.5 * DECAY_RANK ** -0.5 * nrm(ks[15], (L, 2, DECAY_RANK, R_WIDTH), f32),
        "rwkv_a0": 0.5 * nrm(ks[16], (L, 2, R_WIDTH), f32),
        "rwkv_a2": 0.5 * ICLR_RANK ** -0.5 * nrm(ks[17], (L, 2, ICLR_RANK, R_WIDTH), f32),
        "rwkv_g2": GATE_RANK ** -0.5 * nrm(ks[18], (L, GATE_RANK, R_WIDTH), f32),
        "rwkv_k_k": 1.0 + 0.1 * nrm(ks[19], (L, R_WIDTH), f32),
        "rwkv_k_a": 1.0 + 0.1 * nrm(ks[20], (L, R_WIDTH), f32),
        "rwkv_r_k": 0.1 * nrm(ks[21], (L, R_HEADS, R_HEAD_DIM), f32),
        "rwkv_ln_g": 1.0 + 0.02 * nrm(ks[22], (L, R_WIDTH), f32),
        "rwkv_ln_b": 0.02 * nrm(ks[23], (L, R_WIDTH), f32),
        "w_attn_br": ATTN_WIDTH ** -0.5 * nrm(ks[24], (L, ATTN_WIDTH, D_MODEL), f32),
        "w_rwkv_br": R_WIDTH ** -0.5 * nrm(ks[25], (L, R_WIDTH, D_MODEL), f32),
        "w_out": D_MODEL ** -0.5 * nrm(ks[26], (L, D_MODEL, D_MODEL), f32),
        "norm2_g": 1.0 + 0.02 * nrm(ks[27], (L, D_MODEL), f32),
        "ffn_up": D_MODEL ** -0.5 * nrm(ks[28], (L, D_MODEL, 2 * D_FF), f32),
        "ffn_conv": conv_base + 0.1 * nrm(ks[29], (L, 3, 2 * D_FF), f32),
        "ffn_down": D_FF ** -0.5 * nrm(ks[30], (L, D_FF, D_MODEL), f32),
        "final_norm_g": 1.0 + 0.02 * nrm(ks[31], (D_MODEL,), f32),
    }

def reference(x_prompt, x_sample, cache_k, cache_v, state_rwkv, c, c_ctx,
              w_ada, b_ada, norm1_g, w_in, q_norm_g, k_norm_g, rwkv_conv,
              rwkv_w0, rwkv_w2, rwkv_a0, rwkv_a2, rwkv_g2, rwkv_k_k, rwkv_k_a,
              rwkv_r_k, rwkv_ln_g, rwkv_ln_b, w_attn_br, w_rwkv_br, w_out,
              norm2_g, ffn_up, ffn_conv, ffn_down, final_norm_g):
    rows = x_sample.shape[1] // GRID_W
    rope = _axial_rope_tables(rows)
    s_zero = jnp.zeros((x_prompt.shape[0], 2, R_HEADS, R_HEAD_DIM, R_HEAD_DIM), jnp.float32)
    xp, xs = x_prompt, x_sample
    new_k, new_v, new_s = [], [], []
    for l in range(DEPTH):
        p = {
            "norm1_g": norm1_g[l], "w_in": w_in[l], "q_norm_g": q_norm_g[l],
            "k_norm_g": k_norm_g[l], "rwkv_conv": rwkv_conv[l], "rwkv_w0": rwkv_w0[l],
            "rwkv_w2": rwkv_w2[l], "rwkv_a0": rwkv_a0[l], "rwkv_a2": rwkv_a2[l],
            "rwkv_g2": rwkv_g2[l], "rwkv_k_k": rwkv_k_k[l], "rwkv_k_a": rwkv_k_a[l],
            "rwkv_r_k": rwkv_r_k[l], "rwkv_ln_g": rwkv_ln_g[l], "rwkv_ln_b": rwkv_ln_b[l],
            "w_attn_br": w_attn_br[l], "w_rwkv_br": w_rwkv_br[l], "w_out": w_out[l],
            "norm2_g": norm2_g[l], "ffn_up": ffn_up[l], "ffn_conv": ffn_conv[l],
            "ffn_down": ffn_down[l],
        }
        mod_ctx = (jax.nn.silu(c_ctx) @ w_ada[l] + b_ada[l])[None, :]
        mod_lat = jax.nn.silu(c) @ w_ada[l] + b_ada[l]
        xp, k_ctx, v_ctx, s_ctx = _layer(xp, mod_ctx, p, None, None, None, s_zero)
        new_k.append(k_ctx)
        new_v.append(v_ctx)
        new_s.append(s_ctx)
        xs, _, _, _ = _layer(xs, mod_lat, p, rope, cache_k[:, l], cache_v[:, l], state_rwkv[:, l])
    y_prompt = _rmsnorm(xp, final_norm_g)
    y_sample = _rmsnorm(xs, final_norm_g)
    new_cache_k = jnp.stack(new_k, axis=1)
    new_cache_v = jnp.stack(new_v, axis=1)
    new_state_rwkv = jnp.stack(new_s, axis=1)
    return (y_prompt, y_sample, new_cache_k, new_cache_v, new_state_rwkv)


_drawn_inputs = setup_inputs


def setup_inputs(seed=0):
    import zlib

    import numpy as np

    out = dict(_drawn_inputs(seed))
    spreads = {}
    factors = {'cache_k': 8.0,
     'cache_v': 8.0,
     'state_rwkv': 8.0,
     'q_norm_g': 8.0,
     'k_norm_g': 9.377,
     'rwkv_ln_g': 24.825,
     'rwkv_ln_b': 22.585,
     'norm2_g': 7.935,
     'final_norm_g': 8.353}
    for name, (base, spread) in spreads.items():
        noise = np.random.default_rng([zlib.crc32(name.encode()), seed]).standard_normal(out[name].shape)
        drawn = base * np.exp(spread * noise) if base else spread * noise
        out[name] = __import__('jax').numpy.asarray(drawn.astype(out[name].dtype))
    for name, factor in factors.items():
        out[name] = (out[name] * factor).astype(out[name].dtype)
    return out
```

```python
from contextlib import ExitStack

import numpy as np

import concourse.bass as bass
from concourse import mybir

ALU = mybir.AluOpType
ACT = mybir.ActivationFunctionType
F32 = mybir.dt.float32
F32R = mybir.dt.float32r
AX = mybir.AxisListType.X
ds = bass.ds

P = 128
D = 1024
KD = D // P
T = 640
LAT, CTX = 512, 128
TP = 644
L0, C0 = 1, 514
HALF = TP // 2
FLAT = 512 - HALF
NT = T // P
NU = 14
FF = 22
NBLK_U, NBLK_Q, NBLK_G = 7, 3, 8
BLK_BR = NBLK_U + NBLK_Q + NBLK_G
BLK_OUT = BLK_BR + 4
BLK_UP = BLK_OUT + 4
NBLK = BLK_UP + FF
WEL = KD * 256
LEVELS = (2, 4, 8, 16, 32, 64)
EHALF = float(np.exp(-0.5)) / 2
EPS, GN_EPS = 1e-6, 64e-5
STEPS_RWKV = 60
ADA_EARLY = 4


def columns():
    at, n = {}, 0
    for name, w in (("c", 16), ("bada", 48), ("g1", 8), ("g2", 8), ("gf", 8), ("qg", 1), ("kg", 1),
                    ("rconv", NU * 3), ("fconv", 2 * FF * 3), ("w0", 8), ("a0", 8), ("kk", 4), ("ka", 4),
                    ("rk", 4), ("lng", 4), ("lnb", 4)):
        at[name] = n
        n += w
    return at, n


def const_columns():
    at, n = {}, 0
    for name, w in (("ident", P), ("ones", P), ("blk", P), ("rot", P), ("sii", P), ("mar", 4 * P),
                    ("m1t", 2 * P), ("lev", len(LEVELS) * 2 * P), ("reset", T), ("cos", LAT), ("sin", LAT)):
        at[name] = n
        n += w
    return at, n


def constants():
    at, n = const_columns()
    out = np.zeros((P, n), np.float32)

    def put(name, a):
        out[:, at[name]:at[name] + a.reshape(P, -1).shape[1]] = a.reshape(P, -1)

    i = np.arange(P)
    r, c = i[:, None], i[None, :]
    put("ident", (r == c) * 1.0)
    put("ones", np.ones((P, P)))
    put("blk", (r // 64 == c // 64) * 1.0)
    rot = np.zeros((P, P))
    for m in range(P):
        if m % 64 < 32:
            rot[m + 32, m] = -1.0
        else:
            rot[m - 32, m] = 1.0
    put("rot", rot)
    sii = np.zeros((P, 2, 64))
    sii[64 + np.arange(64), 0, np.arange(64)] = 1.0
    sii[np.arange(64), 1, np.arange(64)] = 1.0
    put("sii", sii)
    put("mar", np.stack([np.stack([r < c, r <= c], 1), np.stack([r > c, r >= c], 1)], 1) * 1.0)
    put("m1t", np.stack([(r // 2 == c // 2) & (r < c), (r // 2 == c // 2) & (r > c)], 1) * 1.0)
    lev = []
    for m in LEVELS:
        same = r // (2 * m) == c // (2 * m)
        low = same & (r % (2 * m) >= m) & (c % (2 * m) < m)
        lev.append(np.stack([same & (r % (2 * m) < m) & (c % (2 * m) >= m), low], 1))
    put("lev", np.stack(lev, 1) * 1.0)
    put("reset", np.broadcast_to((np.arange(T) % P != 0) * 1.0, (P, T)))
    f32 = np.float32
    row = np.repeat(np.arange(LAT // 64), 64).astype(f32)
    col = np.tile(np.arange(64), LAT // 64).astype(f32)
    inv = (1.0 / (f32(10000.0) ** (np.arange(16, dtype=f32) / f32(16)))).astype(f32)
    ang = np.concatenate([row[:, None] * inv, col[:, None] * inv], -1).astype(f32)
    put("cos", np.cos(ang).T[i % 32])
    put("sin", np.sin(ang).T[i % 32])
    return out


class Steps:

    def __init__(self, eng, sem):
        self.eng, self.sem, self.base, self.n = eng, sem, 0, 0

    def do(self, ins):
        ins.then_inc(self.sem, 1)
        self.n += 1
        return self.n

    def need(self, mark):
        self.eng.wait_ge(self.sem, self.base + mark)

    def last(self, ins):
        self.need(self.do(ins))

    def enter(self, i, per):
        self.before, self.per = self.n + 0, per
        self.kept = self.base
        self.base, self.n = self.base + self.before + i * per, 0

    def leave(self, times):
        assert self.n == self.per, (self.n, self.per)
        self.base, self.n = self.kept, self.before + times * self.per


def build(nc, io):
    PC, npar = columns()
    CC, ncon = const_columns()
    out_names = io["outs"]
    par_d, con_d, x_d, wada_d, wblk_d, wdn_d = (io[k] for k in ("par", "con", "x", "wada", "wblk", "wdn"))
    ck_d, cv_d, hpw_d = (io[k] for k in ("ck", "cv", "hpw"))
    y_d, nk_d, nv_d, ns_d = out_names

    u_s = nc.dram_tensor("u_scratch", [12, P, T], F32, kind="Internal").ap()
    gate_s = nc.dram_tensor("gate_scratch", [KD, P, 2, TP], F32, kind="Internal").ap()
    br_s = nc.dram_tensor("branch_scratch", [8, P, TP], F32, kind="Internal").ap()

    ctx = ExitStack()
    ctx.enter_context(nc.allow_non_contiguous_dma(reason="small layouts"))
    spot = [16512]
    top = 229344

    def sb(name, shape, dt=F32):
        n = 4 * int(np.prod(shape[1:]))
        t = nc.alloc_sbuf_tensor_at(name, shape, dt, offset=spot[0])
        spot[0] += (n + 31) // 32 * 32
        assert spot[0] <= top, (name, spot[0])
        return t

    def sem(name):
        return ctx.enter_context(nc.semaphore(name))

    ps = ctx.enter_context(nc.psum_tensor("ps", [P, 8, 512], F32))
    psf = ps[:, :, :].rearrange("p b n -> p (b n)")

    def bank(b, n=512, off=0):
        return psf[:, b * 512 + off:b * 512 + off + n]

    par = sb("par", [P, npar])
    con = sb("con", [P, ncon])
    onesr = sb("onesr", [P, P], F32R)
    modT = sb("modT", [P, 48, 2])
    sc1g = sb("sc1g", [P, KD, 2])
    sc2g = sb("sc2g", [P, KD, 2])
    g1h = sb("g1h", [P, KD, 2])
    g2h = sb("g2h", [P, KD, 2])
    silu_c = sb("silu_c", [P, KD, 2])
    hw0 = sb("hw0", [P, 4, 2])
    ha0 = sb("ha0", [P, 4, 2])
    kac = sb("kac", [P, 2, 4])
    qg8 = sb("qg8", [P, 1])
    raw_at = spot[0]
    raw = [sb(f"raw{s}", [P, WEL]) for s in range(2)]
    after_raw, spot[0] = spot[0], raw_at
    al = [[sb(f"al{s}_{r}", [P, 2, 2, P]) for r in range(4)] for s in range(2)]
    assert spot[0] <= after_raw
    spot[0] = after_raw
    common = spot[0]
    whi = [sb(f"whi{s}", [P, WEL], F32R) for s in range(2)]
    wlo = [sb(f"wlo{s}", [P, WEL], F32R) for s in range(2)]
    after_ring = spot[0]
    sqf = [sb(f"sqf{s}", [P, TP]) for s in range(2)]
    sqh = [sb(f"sqh{s}", [P, TP], F32R) for s in range(2)]
    sql = [sb(f"sql{s}", [P, TP], F32R) for s in range(2)]
    hf = [sb(f"hf{s}", [P, TP]) for s in range(2)]
    rs = sb("rs", [P, TP])
    xr = sqf
    norm_end = spot[0]
    hhi = [sb(f"hhi{k}", [P, TP], F32R) for k in range(KD)]
    hlo = [sb(f"hlo{k}", [P, TP], F32R) for k in range(KD)]
    h_end = spot[0]
    xT = sb("xT", [P, KD, TP])
    modrow = sb("modrow", [2, 512 * ADA_EARLY])
    spot[0] = common
    adaw = [sb(f"adaw{s}", [P, KD, 512]) for s in range(2)]
    assert spot[0] <= after_ring
    spot[0] = top - 4 * (6 * TP + 2 * T)
    qkv = sb("qkv", [P, 6, TP])
    keep_u = spot[0]
    wdad = sb("wdad", [P, T])
    gdT = sb("gdT", [P, T])
    spot[0] = h_end
    craw = [sb(f"craw{s}", [P, TP]) for s in range(2)]
    cacc = [sb(f"cacc{s}", [P, TP]) for s in range(2)]
    uout = [sb(f"uout{s}", [P, T]) for s in range(2)]
    gout = [sb(f"gout{s}", [P, TP]) for s in range(2)]
    assert spot[0] <= top - 4 * (6 * TP + 2 * T)
    spot[0] = common
    k2 = sb("k2", [64, 2, 768])
    kst = sb("kst", [P, 2, 2, 768], F32R)
    qst = [sb(f"qst{h}", [P, 4, LAT], F32R) for h in range(2)]
    k2c = sb("k2c", [P, 2, P])
    vt = sb("vt", [P, 7, P])
    asq = [sb(f"asq{s}", [P, TP]) for s in range(2)]
    arn = [sb(f"arn{s}", [P, TP]) for s in range(2)]
    rt1 = sb("rt1", [P, LAT])
    rt2 = sb("rt2", [P, LAT])
    pr = [sb(f"pr{s}", [P, 768]) for s in range(2)]
    pt = [sb(f"pt{s}", [P, 6, LAT]) for s in range(2)]
    rdiag = [sb(f"rdiag{s}", [P, P]) for s in range(2)]
    nmax = sb("nmax", [P, 40])
    lsum = sb("lsum", [P, 40])
    rsum = sb("rsum", [P, 40])
    prc = sb("prc", [P, 2, 4, P])
    ptc = sb("ptc", [P, 2, 4, P])
    aT = sb("aT", [P, 4, TP])
    assert spot[0] <= top - 4 * (6 * TP + 2 * T)
    spot[0] = common
    uc = [sb(f"uc{s}", [P, 3, T]) for s in range(2)]
    hpw = [sb(f"hpw{s}", [P, 4 * P]) for s in range(2)]
    wcur = [w[:, 0:2 * P].rearrange("p (d n) -> p d n", d=2) for w in hpw]
    gcur = [w[:, 2 * P:3 * P] for w in hpw]
    stv = [w[:, 3 * P:4 * P].rearrange("p (d n) -> p d n", d=2) for w in hpw]
    stf = [sb(f"stf{s}", [P, 2, 64]) for s in range(2)]
    stx = [sb(f"stx{s}", [P, 2, 2, 64]) for s in range(2)]
    ar = [sb(f"ar{s}", [P, 2, NT, 2, 2, P]) for s in range(2)]
    bt = [sb(f"bt{s}", [P, 2, T]) for s in range(2)]
    kt_at = spot[0]
    kt = [sb(f"kt{s}", [P, 2, T]) for s in range(2)]
    after_kt, spot[0] = spot[0], kt_at
    rwo = [sb(f"rwo{s}", [P, TP]) for s in range(2)]
    spot[0] = after_kt
    ksum = [sb(f"ksum{s}", [P, T]) for s in range(2)]
    ecin = [sb(f"ecin{s}", [P, 2, NT]) for s in range(2)]
    ecol = [sb(f"ecol{s}", [P, 3, 2, NT]) for s in range(2)]
    si = [sb(f"si{s}", [P, NT, 2, 2, 64]) for s in range(2)]
    vz = [sb(f"vz{s}", [P, 4, 64]) for s in range(2)]
    akm, abm, tm, rm, hm, xa, bkt, ep = [], [], [], [], [], [], [], []
    kfc = [sb(f"kfc{s}", [P, 2]) for s in range(2)]
    chunk_at = spot[0]
    for s in range(2):
        slot_at = spot[0]
        akm.append(sb(f"akm{s}", [P, 2, 2, 2, P]))
        abm.append(sb(f"abm{s}", [P, 2, 2, 2, P]))
        tm.append(sb(f"tm{s}", [P, 2, 2, P]))
        rm.append(sb(f"rm{s}", [P, 2, 2, P]))
        hm.append(sb(f"hm{s}", [P, 2, 2, P]))
        xa.append(sb(f"xa{s}", [P, 2, 4, 64]))
        bkt.append(sb(f"bkt{s}", [P, 2, 2, P]))
        slot_end = spot[0]
        spot[0] = slot_at
        ep.append([sb(f"ep{s}_{j}", [P, T]) for j in range(4)])
        spot[0] = slot_end
    chunk_end = spot[0]
    spot[0] = chunk_at
    adl = [sb(f"adl{s}", [P, KD, 512]) for s in range(2)]
    adrow = [sb(f"adrow{s}", [2, 512]) for s in range(2)]
    assert spot[0] <= chunk_end
    spot[0] = chunk_end
    wu = [h[:, :, :, :].rearrange("p d h (b n) -> p d (h b) n", b=2) for h in hm]
    temps_at = spot[0]
    qy = [sb(f"qy{s}", [P, NT, 2, 2, P]) for s in range(2)]
    mn = [sb(f"mn{s}", [P, NT, 4, 64]) for s in range(2)]
    assert spot[0] <= keep_u, (spot[0], keep_u)
    spot[0] = temps_at
    tb = [sb(f"tb{j}", [P, T]) for j in range(12)]
    assert spot[0] <= keep_u, (spot[0], keep_u)
    rn = [tb[1], tb[11]]
    spot[0] = after_ring
    bhi = [sb(f"bhi{k}", [P, TP], F32R) for k in range(8)]
    blo = [sb(f"blo{k}", [P, TP], F32R) for k in range(8)]
    bld = [sb(f"bld{s}", [P, TP]) for s in range(8)]
    gld = [sb(f"gld{s}", [P, 2, TP]) for s in range(2)]
    m1 = [sb(f"m1_{s}", [P, TP]) for s in range(2)]
    m2 = [sb(f"m2_{s}", [P, TP]) for s in range(2)]
    mhi = [sb(f"mhi{k}", [P, TP], F32R) for k in range(KD)]
    mlo = [sb(f"mlo{k}", [P, TP], F32R) for k in range(KD)]
    spot[0] = norm_end
    x1 = sb("x1", [P, KD, TP])
    x1_end = spot[0]
    h2hi = [sb(f"h2hi{k}", [P, TP], F32R) for k in range(KD)]
    h2lo = [sb(f"h2lo{k}", [P, TP], F32R) for k in range(KD)]
    af = sb("af", [P, FF, TP - 2])
    spot[0] = after_ring
    fraw = [sb(f"fraw{s}", [P, TP]) for s in range(2)]
    facc = [sb(f"facc{s}", [P, TP]) for s in range(2)]
    fcu = sb("fcu", [P, TP - 2])
    fcg = sb("fcg", [P, TP - 2])
    ftg = sb("ftg", [P, TP - 2])
    assert spot[0] <= norm_end
    spot[0] = x1_end
    dhi = [sb(f"dhi{s}", [P, TP - 2], F32R) for s in range(2)]
    dlo = [sb(f"dlo{s}", [P, TP - 2], F32R) for s in range(2)]
    yout = [sb(f"yout{s}", [P, TP]) for s in range(2)]

    def cc(name, n=P):
        return con[:, CC[name]:CC[name] + n]

    ident, blk1, rotm, ones = cc("ident"), cc("blk"), cc("rot"), cc("ones")
    sii = cc("sii").rearrange("p (h n) -> p h n", h=2)
    mar = cc("mar", 4 * P).rearrange("p (d a n) -> p d a n", d=2, a=2)
    m1t = cc("m1t", 2 * P).rearrange("p (d n) -> p d n", d=2)
    lev = cc("lev", len(LEVELS) * 2 * P).rearrange("p (l d n) -> p l d n", l=len(LEVELS), d=2)
    reset, cosT, sinT = cc("reset", T), cc("cos", LAT), cc("sin", LAT)

    def pc(name, i=0, n=1):
        return par[:, ds(PC[name] + i, n)]

    def halves(ap, n=TP):
        return ap[:, 0:HALF], ap[:, HALF:n]

    def out_halves(b, n=TP):
        at = b * 512 + FLAT
        return psf[:, at:at + HALF], psf[:, at + HALF:at + n]

    def tile(b, n=TP):
        return psf[:, b * 512 + FLAT:b * 512 + FLAT + n]

    def by_tile(ap):
        return ap.rearrange("p (t n) -> p t n", t=NT)

    def own_columns(b):
        return bank(b).rearrange("p (d x n) -> p d x n", d=2, x=4)[:, :, 0:4:3, :]

    par_ld, con_ld, x_ld = sem("par_loaded"), sem("constants_loaded"), sem("x_loaded")
    ada_ld = [sem(f"ada_loaded{s}") for s in range(2)]
    w_ld = [sem(f"weights_loaded{s}") for s in range(2)]
    hi_done, lo_done = sem("weights_hi_split"), sem("weights_lo_split")
    tile_done, tile_evac = sem("product_tile_done"), sem("product_tile_read")
    conv_done = sem("convolved")
    sq_done, sqs_done, sq_used, rs_done = sem("squares_ready"), sem("squares_split"), sem("squares_summed"), sem("rsqrt_ready")
    hh_done = sem("modulated_hi")
    xr_done, hf_done, h_done = sem("normalized"), sem("modulated"), sem("modulated_split")
    ctanh_done, silu_done = sem("silu_tanh"), sem("silu_ready")
    ada_done, row_done, modt_done = sem("mod_row_product"), sem("mod_row_copied"), sem("mod_turned")
    mod_done, setup_done = sem("mod_ready"), sem("derived_ready")
    dve, act, pool = sem("vector_steps"), sem("scalar_steps"), sem("pool_steps")
    barrier = sem("phase_over")
    u_st = [sem(f"u_stored{s}") for s in range(2)]
    g_st = [sem(f"gates_stored{s}") for s in range(2)]
    kv_st, a_st = sem("new_kv_stored"), sem("attention_stored")
    cache_ld = sem("cache_loaded")
    asq_done, ass_done, arn_done, aqn_done, arot_done, aq_done = (
        sem("q_squares"), sem("q_square_sums"), sem("q_rsqrt"), sem("q_normed"), sem("q_rotated"), sem("q_roped"))
    vt_done, vt_copied = sem("v_turned"), sem("v_copied")
    qst_done, pt_copied_a = sem("qk_parts"), sem("probs_copied_by_scalar")
    s_done, max_done, exp_done, prob_done, pt_done, pt_copied, o_done, o_copied = (
        sem("scores"), sem("score_max"), sem("exponentials"), sem("probabilities"), sem("probs_turned"),
        sem("probs_copied"), sem("head_out"), sem("head_out_copied"))
    rw_ld = [sem(f"rwkv_loaded{s}") for s in range(2)]
    low_done = sem("decay_gate_inputs")
    prep_read = sem("prep_products_read")
    pe_prep, ac_prep, dv_prep = sem("prep_products"), sem("prep_scalar"), sem("prep_vector")
    pe_g = [sem(f"chunk_products{s}") for s in range(2)]
    dv_g = [sem(f"chunk_vector{s}") for s in range(2)]
    ac_g = [sem(f"chunk_scalar{s}") for s in range(2)]
    po_g = [sem(f"chunk_levels{s}") for s in range(2)]
    pe_s, dv_s = sem("state_products"), sem("state_vector")
    pe_e = [sem(f"epilogue_products{s}") for s in range(2)]
    dv_e = [sem(f"epilogue_vector{s}") for s in range(2)]
    ac_e = [sem(f"epilogue_scalar{s}") for s in range(2)]
    ln_done = sem("variance_log")
    rwo_done, pl_prep, kf_done = sem("rwkv_out"), sem("prep_pool"), sem("key_factor")
    rw_st = [sem(f"rwkv_stored{s}") for s in range(2)]
    ns_st = [sem(f"state_stored{s}") for s in range(2)]
    b_ld = [sem(f"branch_loaded{s}") for s in range(8)]
    gl_ld = [sem(f"gates_loaded{s}") for s in range(2)]
    b_hi, b_lo = sem("branch_hi"), sem("branch_lo")
    mf_done, m_hi, m_lo = sem("merged"), sem("merged_hi"), sem("merged_lo")
    x1_ld = sem("x_again_loaded")
    tg_done, act_done = sem("gate_tanh"), sem("ffn_activated")
    wd_ld = [sem(f"down_loaded{s}") for s in range(2)]
    d_hi, d_lo, d_used, d_evac = sem("down_hi"), sem("down_lo"), sem("down_used"), sem("down_read")
    yo_done, y_st = sem("y_ready"), [sem(f"y_stored{s}") for s in range(2)]

    block = ctx.enter_context(nc.Block())

    def phase_over(eng, n):
        eng.drain().then_inc(barrier, 1)
        eng.wait_ge(barrier, 4 * n)

    NL = len(LEVELS)
    PE_ST = ["KAB", "TR", "H0", "X0", "G0"] + [f"{x}{l}" for l in range(1, NL) for x in "HG"] + ["WU", "QY", "MN"]
    DV_ST = ["AK", "AB", "R0"] + [f"{x}{l}" for l in range(NL - 1) for x in "UV"] + [f"V{NL - 1}", "QY"]
    AC_ST = ["TR", "E0", "X0"] + [f"E{l}" for l in range(1, NL)] + ["WU", "QY", "MN"]
    PO_ST = [f"A{l}" for l in range(NL)]

    COST = {"KAB": 4.0, "TR": 3.0, "X0": 1.0, "WU": 1.5, "QY": 2.0, "MN": 2.0}
    SKEW = 1.0
    begins, clock = {}, 0.0
    for t in range(NT):
        for name in PE_ST:
            for s in range(2):
                begins[t, name, s] = clock + s * SKEW
            clock += COST.get(name, 2.3)

    def in_order(names):
        cause = {"AK": "KAB", "AB": "KAB", "R0": "KAB"}

        def key(stage):
            t, name, s = stage
            by = name if name in PE_ST else cause.get(name) or {"E": "H", "U": "G", "V": "G"}[name[0]] + name[1]
            return begins[t, by, s], s

        return sorted(((t, name, s) for t in range(NT) for name in names for s in range(2)), key=key)

    def at_stage(names, it, t, name):
        return (it * NT + t) * len(names) + names.index(name) + 1

    @block.sync
    def _(sp):
        sp.dma_start(par[:, :], par_d).then_inc(par_ld, 16)
        sp.dma_start(adaw[0][:, :, :], wada_d[0]).then_inc(ada_ld[0], 16)
        sp.dma_start(xT[:, :, :], x_d).then_inc(x_ld, 16)
        sp.dma_start(adaw[1][:, :, :], wada_d[1]).then_inc(ada_ld[1], 16)
        for n in range(2, ADA_EARLY):
            sp.wait_ge(ada_done, n - 1)
            sp.dma_start(adaw[n % 2][:, :, :], wada_d[n]).then_inc(ada_ld[n % 2], 16)
        sp.dma_start(con[:, :], con_d).then_inc(con_ld, 16)
        for s in range(2):
            sp.dma_start(raw[s][:, :], wblk_d[s]).then_inc(w_ld[s], 16)
        with sp.Fori(1, BLK_BR // 2) as i:
            for s in range(2):
                sp.wait_ge(hi_done, 2 * i + s - 1)
                sp.wait_ge(lo_done, 2 * i + s - 1)
                sp.dma_start(raw[s][:, :], wblk_d[2 * i + s]).then_inc(w_ld[s], 16)
        sp.wait_ge(barrier, 12)
        u_of = u_s.rearrange("(j h) p n -> h p j n", j=3)
        for it in range(2):
            for s in range(2):
                if it:
                    sp.wait_ge(rwo_done, s + 1)
                    sp.dma_start(br_s[s + 4], rwo[s][:, :]).then_inc(rw_st[s], 16)
                sp.dma_start(hpw[s][:, :], hpw_d[2 * it + s]).then_inc(rw_ld[s], 16)
            for s in range(2):
                if it:
                    sp.wait_ge(rw_st[s], 16)
                    sp.wait_ge(ns_st[s], 16)
                sp.dma_start(uc[s][:, :, :], u_of[2 * it + s]).then_inc(rw_ld[s], 16)
            for m in range(4):
                n = 4 * it + ADA_EARLY + m
                sp.wait_ge(ada_done, n - 1)
                sp.dma_start(adl[m % 2][:, :, :], wada_d[n]).then_inc(ada_ld[m % 2], 16)
            for s in range(2):
                sp.wait_ge(dv_s, 10 * it + s + 1)
                sp.dma_start(ns_d[2 * it + s], stf[s][:, :, :]).then_inc(ns_st[s], 16)
        for s in range(2):
            for n in range(2):
                sp.wait_ge(pe_s, 8 + n + 1)
            sp.dma_start(raw[s][:, :], wblk_d[BLK_BR + s]).then_inc(w_ld[s], 16)
        for s in range(2):
            sp.wait_ge(rwo_done, s + 3)
            sp.dma_start(br_s[s + 6], rwo[s][:, :]).then_inc(rw_st[s], 16)
        with sp.Fori(BLK_BR // 2 + 1, NBLK // 2) as i:
            for s in range(2):
                sp.wait_ge(hi_done, 2 * i + s - 1)
                sp.wait_ge(lo_done, 2 * i + s - 1)
                sp.dma_start(raw[s][:, :], wblk_d[2 * i + s]).then_inc(w_ld[s], 16)
        for s in range(2):
            sp.wait_ge(hi_done, NBLK - 1 + s)
            sp.wait_ge(lo_done, NBLK - 1 + s)
            sp.dma_start(raw[s][:, 0:512], wdn_d[s]).then_inc(wd_ld[s], 16)
        with sp.Fori(1, FF) as i:
            for s in range(2):
                sp.wait_ge(d_hi, 2 * i + s - 1)
                sp.wait_ge(d_lo, 2 * i + s - 1)
                sp.dma_start(raw[s][:, 0:512], wdn_d[2 * i + s]).then_inc(wd_ld[s], 16)
        for k in range(KD):
            sp.wait_ge(yo_done, k + 1)
            sp.dma_start(y_d[k], yout[k % 2][:, :]).then_inc(y_st[k % 2], 16)
        for s in range(2):
            sp.wait_ge(y_st[s], 16 * KD // 2)
            sp.wait_ge(ns_st[s], 32)

    @block.gpsimd
    def _(gp):
        phase_over(gp, 1)
        for i in range(6):
            for s in range(2):
                gp.wait_ge(conv_done, 2 * i + s + 1)
                gp.dma_start(u_s[2 * i + s], uout[s][:, :]).then_inc(u_st[s], 16)
        for i in range(NBLK_G):
            for s in range(2):
                gp.wait_ge(tile_evac, 2 * i + s + 2 * (NBLK_U + NBLK_Q) + 3)
                gp.dma_start(gate_s[i, :, s, :], gout[s][:, :]).then_inc(g_st[s], 16)
        for s in range(2):
            gp.wait_ge(u_st[s], 16 * 6)
            gp.wait_ge(g_st[s], 16 * NBLK_G)
        phase_over(gp, 2)
        for kv in range(2):
            gp.dma_start(k2[:, kv, 512:768], ck_d[kv]).then_inc(cache_ld, 16)
        gp.dma_start(vt[:, 4:6, :], cv_d).then_inc(cache_ld, 16)
        gp.wait_ge(aqn_done, 5)
        gp.dma_start(nk_d, qkv[:, 4, C0:C0 + CTX]).then_inc(kv_st, 16)
        gp.dma_start(nv_d, qkv[:, 5, C0:C0 + CTX]).then_inc(kv_st, 16)
        gp.wait_ge(o_copied, 10)
        gp.dma_start(br_s[0:4].rearrange("k p n -> p k n"), aT[:, :, :]).then_inc(a_st, 16)
        gp.wait_ge(kv_st, 32)
        gp.wait_ge(a_st, 16)
        phase_over(gp, 3)
        st = Steps(gp, pool)
        for s in range(2):
            ins = gp.memset(ar[s][:, :, :, :, :, :].rearrange("p d t h a n -> p (d t h a n)"), 0.0)
            for t in range(NT):
                ins = gp.tensor_copy(si[s][:, t], sii.unsqueeze(1).broadcast_to([P, 2, 2, 64]))
        ins.then_inc(pl_prep, 1)
        gp.wait_ge(pl_prep, 1)
        with gp.Fori(0, 2) as it:
            st.enter(it, 4)
            for s in range(2):
                for d in range(2):
                    gp.wait_ge(ac_prep, 8 * it + 2 * s + 5 + d)
                    for h in range(2):
                        rows = slice(64 * h, 64 * h + 64)
                        ins = gp.tensor_tensor(ar[s][rows, d, :, h, 1, :], by_tile(uc[s][rows, 0, :]), by_tile(tb[9][rows, :]), ALU.mult)
                        if h == 0:
                            st.last(ins)
                    ins.then_inc(pl_prep, 1)
                    gp.wait_ge(pl_prep, 4 * it + 2 * s + d + 2)
            for t in range(NT):
                for l in range(NL):
                    for s in range(2):
                        if l == 0:
                            gp.wait_ge(dv_g[s], at_stage(DV_ST, it, t, "AB"))
                        n = NL * t + l - 4
                        if n >= 0:
                            gp.wait_ge(pe_g[s], at_stage(PE_ST, it, n // NL, f"H{n % NL}"))
                        gp.tensor_tensor(al[s][(NL * t + l) % 4][:, :, :, :], abm[s][:, :, :, 0, :],
                                         lev[:, l].unsqueeze(2).broadcast_to([P, 2, 2, P]), ALU.mult).then_inc(po_g[s], 1)
            st.leave(2)
        for s in range(2):
            gp.wait_ge(rw_st[s], 32)
        phase_over(gp, 4)
        for k in range(8):
            gp.dma_start(bld[k][:, :], br_s[k]).then_inc(b_ld[k], 16)
        for f in range(KD):
            if f >= 2:
                gp.wait_ge(mf_done, f - 1)
            gp.dma_start(gld[f % 2][:, :, :], gate_s[f]).then_inc(gl_ld[f % 2], 16)
        gp.wait_ge(tile_done, 2 * BLK_OUT)
        gp.wait_ge(mf_done, KD)
        gp.wait_ge(m_lo, KD)
        gp.dma_start(x1[:, :, :], x_d).then_inc(x1_ld, 16)
        phase_over(gp, 5)

    @block.tensor
    def _(pe):
        def sum_squares(n):
            outs = out_halves(4)
            for k in range(KD):
                pe.wait_ge(sqs_done, n * KD + k + 1)
                for j, part in enumerate((sqh[k % 2], sql[k % 2])):
                    for o, x in zip(outs, halves(part)):
                        mm = pe.matmul(o, onesr[:, :], x, start=(k == 0 and j == 0), stop=(k == KD - 1 and j == 1))
                mm.then_inc(sq_used, 1)

        def dense_tile(s, j, ks, xh, xl, outs, width, stop=True):
            for n, k in enumerate(ks):
                hi = whi[s][:, k * width + j * P:k * width + j * P + P]
                lo = wlo[s][:, k * width + j * P:k * width + j * P + P]
                first, last = n == 0, n == len(ks) - 1
                for w, x in ((hi, xl[n]), (lo, xh[n]), (hi, xh[n])):
                    for o, v in zip(outs, halves(x)):
                        mm = pe.matmul(o, w, v, start=first, stop=last and w is hi and x is xh[n])
                    first = False
            return mm

        def dense_block(b, s, xh, xl):
            for j in range(2):
                if j == 0:
                    pe.wait_ge(lo_done, b + 1)
                    pe.wait_ge(hi_done, b + 1)
                pe.wait_ge(tile_evac, 2 * b + j + 1)
                dense_tile(s, j, range(KD), xh, xl, out_halves(2 * j), 256).then_inc(tile_done, 1)

        def ada_block(n, s, w, b):
            pe.wait_ge(ada_ld[s], 8 * (n - s) + 16)
            pe.wait_ge(row_done, n + 1)
            for k in range(KD):
                mm = pe.matmul(bank(b + s)[0:2], silu_c[:, k, :], w[s][:, k, :], start=(k == 0), stop=(k == KD - 1))
            mm.then_inc(ada_done, 1)

        def ada_turn(n, m):
            pe.wait_ge(row_done, n + 3)
            for j in range(4):
                mm = pe.matmul(bank(6, 2, 8 * m + 2 * j), adrow[m % 2][0:2, j * P:j * P + P], ident[0:2, 0:2], start=True,
                               stop=True)
            mm.then_inc(modt_done, 1)

        pe.wait_ge(silu_done, 1)
        pe.wait_ge(setup_done, 1)
        sum_squares(0)
        for n in range(ADA_EARLY):
            ada_block(n, n % 2, adaw, 2)
        pe.wait_ge(row_done, ADA_EARLY + 2)
        pe.wait_ge(con_ld, 16)
        for j in range(4 * ADA_EARLY):
            mm = pe.transpose(bank(6, 2, 2 * j), modrow[0:2, j * P:j * P + P], ident[0:2, 0:2])
        mm.then_inc(modt_done, ADA_EARLY - 1)
        phase_over(pe, 1)
        pe.wait_ge(h_done, KD)
        with pe.Fori(0, BLK_BR // 2) as i:
            for s in range(2):
                dense_block(2 * i + s, s, hhi, hlo)
        phase_over(pe, 2)
        def rotate(j):
            pe.wait_ge(aqn_done, j + 1)
            if j >= 2:
                pe.wait_ge(aq_done, j - 1)
            pe.matmul(bank(4 + j % 2), rotm, qkv[:, j, L0:L0 + LAT], start=True, stop=True).then_inc(arot_done, 1)

        for j in range(5):
            at = 1024 * (j % 2)
            pe.wait_ge(asq_done, j + 1)
            if j >= 2:
                pe.wait_ge(arn_done, j - 1)
            pe.matmul(psf[:, at:at + 512], blk1, asq[j % 2][:, 0:512], start=True, stop=True)
            pe.matmul(psf[:, at + 512:at + TP], blk1, asq[j % 2][:, 512:TP], start=True, stop=True).then_inc(ass_done, 1)
            if j:
                rotate(j - 1)
        rotate(4)
        for t in range(NT):
            src = qkv[:, 5, (L0 + t * P if t < 4 else C0):(L0 + t * P if t < 4 else C0) + P]
            mm = pe.transpose(bank(6 + t // 4, P, P * (t % 4)), src, ident)
        mm.then_inc(vt_done, 1)
        pe.wait_ge(qst_done, 5)
        pe.wait_ge(cache_ld, 48)
        pe.wait_ge(vt_copied, 1)

        def scores(n):
            h, qt = n // 4, n % 4
            if n >= 2:
                pe.wait_ge(exp_done, n - 1)
            q = qst[h % 2][:, h // 2, qt * P:qt * P + P]
            for part in range(2):
                pe.matmul(bank(2 * (n % 2)), q, kst[:, part, h // 4, 0:512], start=part == 0, stop=part == 1)
            for part in range(2):
                mm = pe.matmul(bank(2 * (n % 2) + 1, 256), q, kst[:, part, h // 4, 512:768], start=part == 0, stop=part == 1)
            mm.then_inc(s_done, 1)

        scores(0)
        for n in range(32):
            h, qt = n // 4, n % 4
            if n < 31:
                scores(n + 1)
            pe.wait_ge(prob_done, n + 1)
            if n >= 1:
                pe.wait_ge(pt_copied, n)
                pe.wait_ge(pt_copied_a, n)
            for c in range(6):
                mm = pe.matmul(bank(4 + c // 3, P, P * (c % 3)), pr[n % 2][:, c * P:c * P + P], rdiag[n % 2][:, :],
                               start=True, stop=True)
            mm.then_inc(pt_done, 1)
            if qt == 3:
                pe.wait_ge(pt_copied, n + 1)
                pe.wait_ge(pt_copied_a, n + 1)
                if h >= 2:
                    pe.wait_ge(o_copied, h - 1)
                rows = slice(64 * (h % 2), 64 * (h % 2) + 64)
                for c in range(6):
                    mm = pe.matmul(bank(6 + h % 2)[rows], vt[:, c, 64 * (h // 4):64 * (h // 4) + 64],
                                   pt[h % 2][:, c, :], start=(c == 0), stop=(c == 5))
                mm.then_inc(o_done, 1)
        pe.wait_ge(exp_done, 32)
        for g in range(2):
            for j in range(4):
                h = 4 * g + j
                rows = slice(64 * (h % 2), 64 * (h % 2) + 64)
                mm = pe.matmul(bank(2 * g + j % 2, P, P * (j // 2)), qkv[rows, h // 2, C0:C0 + CTX], k2c[rows, g, :],
                               start=True, stop=True)
            mm.then_inc(s_done, 1)
        for g in range(2):
            pe.wait_ge(prob_done, 33 + g)
            for j in range(4):
                mm = pe.transpose(bank(4 + g, P, P * j), prc[:, g, j, :], ident)
            mm.then_inc(pt_done, 1)
            pe.wait_ge(pt_copied, 33 + g)
            if g == 0:
                pe.wait_ge(o_copied, 8)
            for j in range(4):
                h = 4 * g + j
                rows = slice(64 * (h % 2), 64 * (h % 2) + 64)
                mm = pe.matmul(bank(6 + g, P, P * (j // 2))[rows], vt[:, 6, 64 * g:64 * g + 64], ptc[:, g, j, :],
                               start=True, stop=True)
            mm.then_inc(o_done, 1)
        phase_over(pe, 3)

        def chunk_stage(it, t, s, name):
            b = 4 * s
            tok = slice(t * P, t * P + P)

            def dv(n, tt=t):
                pe.wait_ge(dv_g[s], at_stage(DV_ST, it, tt, n))

            def ac(n, tt=t):
                pe.wait_ge(ac_g[s], at_stage(AC_ST, it, tt, n))

            if name == "KAB":
                if t == 0:
                    pe.wait_ge(dv_prep, 10 * it + 10)
                    pe.wait_ge(mod_done, it + 2)
                    pe.wait_ge(pl_prep, 4 * it + 5)
                else:
                    dv("QY", t - 1)
                    ac("MN", t - 1)
                for n, src in enumerate((kt[s], bt[s])):
                    for d in range(2):
                        for h in range(2):
                            mm = pe.matmul(bank(b + 2 * n + h, 256, 256 * d), src[:, d, tok], ar[s][:, d, t, h, :, :],
                                           start=True, stop=True)
            elif name == "TR":
                dv("AK")
                for d in range(2):
                    pe.matmul(bank(b + 1, P, P * d), ar[s][:, d, t, 0, 0, :], ident, start=True, stop=False)
                    pe.matmul(bank(b + 1, P, P * d), ar[s][:, d, t, 1, 0, :], ident, start=False, stop=True)
                pe.transpose(bank(b + 1, P, 2 * P), uc[s][:, 2, tok], ident)
                dv("AB")
                for d in range(2):
                    for n, src in enumerate((bt[s], kt[s])):
                        mm = pe.transpose(bank(b + 2, P, P * (2 * d + n)), src[:, d, tok], ident)
            elif name[0] == "H":
                l = int(name[1])
                dv("R0" if l == 0 else f"U{l - 1}")
                pe.wait_ge(po_g[s], at_stage(PO_ST, it, t, f"A{l}"))
                for d in range(2):
                    for h in range(2):
                        mm = pe.matmul(bank(b, P, P * (2 * d + h)), al[s][(NL * t + l) % 4][:, d, h, :], tm[s][:, d, h, :],
                                       start=True, stop=True)
            elif name[0] == "G":
                l = int(name[1])
                ac(f"E{l}")
                if l:
                    dv(f"V{l - 1}")
                for d in range(2):
                    for h in range(2):
                        if l < NL - 1:
                            mm = pe.matmul(bank(b + 1, P, P * (2 * d + h)), rm[s][:, d, h, :], hm[s][:, d, h, :],
                                           start=True, stop=True)
                        if l >= NL - 2:
                            mm = pe.matmul(bank(b + 2, P, P * (2 * d + h)), hm[s][:, d, h, :], rm[s][:, d, h, :],
                                           start=True, stop=True)
            elif name == "X0":
                ac("TR")
                for d in range(2):
                    for h in range(2):
                        mm = pe.matmul(bank(b + 3, P, P * (2 * d + h)), akm[s][:, d, h, 0, :], vz[s][:, 1:3, :],
                                       start=True, stop=True)
            elif name == "WU":
                dv(f"V{NL - 1}")
                ac("X0")
                for d in range(2):
                    for h in range(2):
                        mm = pe.matmul(bank(b, P, P * (2 * d + h)), rm[s][:, d, h, :], xa[s][:, d, 2 * h:2 * h + 2, :],
                                       start=True, stop=True)
            elif name == "QY":
                ac("WU")
                for d in range(2):
                    for h in range(2):
                        o = bank(b + 1 + 2 * h, P, P * d)
                        pe.matmul(o, wu[s][:, d, 2 * h:2 * h + 2, :], abm[s][:, d, h, 1, :], start=True, stop=False)
                        mm = pe.matmul(o, vz[s][:, 2 * h:2 * h + 2, :], akm[s][:, d, h, 1, :], start=False, stop=True)
            elif name == "MN":
                for d in range(2):
                    for h in range(2):
                        o = bank(b + 2, P, P * (2 * d + h))
                        pe.matmul(o, wu[s][:, d, 2 * h:2 * h + 2, :], bkt[s][:, d, 0, :], start=True, stop=False)
                        mm = pe.matmul(o, vz[s][:, 2 * h:2 * h + 2, :], bkt[s][:, d, 1, :], start=False, stop=True)
            mm.then_inc(pe_g[s], 1)

        def chunk_outputs(s, tiles):
            mm = None
            for t in tiles:
                for h in range(2):
                    for d in range(2):
                        mm = pe.matmul(bank(4 * s + 2, P, P * t)[64 * h:64 * h + 64], si[s][:, t, d, h, :],
                                       qy[s][:, t, d, h, :], start=(d == 0), stop=(d == 1))
            return mm

        pe.wait_ge(low_done, 1)
        with pe.Fori(0, 2) as it:
            for n in range(10):
                s = n if n < 2 else (n - 2) // 4
                pe.wait_ge(prep_read, 10 * it + n + 1)
                if n < 2:
                    pe.wait_ge(ac_prep, 8 * it + n + 1)
                    w, x = blk1, tb[11 * n][:, :]
                else:
                    pe.wait_ge(rw_ld[s], 32 * it + 32)
                    d, low = (n - 2) % 4 // 2, n % 2
                    rows = slice(64 * low, 64 * low + 64)
                    w, x = wcur[s][rows, d, :], wdad[rows, :]
                at = 1024 * (n % 2)
                pe.matmul(psf[:, at:at + 512], w, x[:, 0:512], start=True, stop=True)
                pe.matmul(psf[:, at + 512:at + T], w, x[:, 512:T], start=True, stop=True).then_inc(pe_prep, 1)
                if n in (5, 9):
                    for m in ((0, 1) if n == 5 else (2, 3)):
                        if m >= 2:
                            ada_turn(4 * it + ADA_EARLY + m - 2, m - 2)
                        ada_block(4 * it + ADA_EARLY + m, m % 2, adl, 4)
            for m in range(2, 4):
                ada_turn(4 * it + ADA_EARLY + m, m)
            for t, name, s in in_order(PE_ST):
                chunk_stage(it, t, s, name)
            for s in range(2):
                pe.wait_ge(ac_g[s], at_stage(AC_ST, it, NT - 1, "MN"))
                pe.wait_ge(dv_g[s], at_stage(DV_ST, it, NT - 1, "QY"))
                for d in range(2):
                    for h in range(2):
                        mm = pe.matmul(bank(4 * s + 3, 64, 64 * d)[64 * h:64 * h + 64], mn[s][:, 4, 2 * d + h, :],
                                       si[s][:, 4, d, h, :], start=True, stop=True)
                mm.then_inc(pe_s, 1)
            for j in range(3):
                for s in range(2):
                    pe.wait_ge(dv_s, 10 * it + 2 + 2 * j + s + 1)
                    for d in range(2):
                        t = j if d == 0 else 3 - j
                        for h in range(2):
                            mm = pe.matmul(bank(4 * s, 64, 64 * d)[64 * h:64 * h + 64], mn[s][:, t, 2 * d + h, :],
                                           si[s][:, t, d, h, :], start=True, stop=True)
                    mm.then_inc(pe_s, 1)
                for s in range(2):
                    chunk_outputs(s, ((4,), (), (1, 2))[j])
            for s in range(2):
                pe.wait_ge(dv_s, 10 * it + 9 + s)
                chunk_outputs(s, (0, 3)).then_inc(pe_e[s], 1)
            for j in range(4):
                for s in range(2):
                    if j == 0:
                        pe.wait_ge(ac_e[s], 3 * it + 1)
                        b, w, x = 0, blk1, ep[s][0][:, :]
                    elif j == 1:
                        pe.wait_ge(ac_e[s], 3 * it + 2)
                        b, w, x = 2, blk1, ep[s][2][:, :]
                    elif j == 2:
                        pe.wait_ge(dv_e[s], 2 * it + 2)
                        b, w, x = 0, blk1, ep[s][3][:, :]
                    else:
                        pe.wait_ge(ac_e[s], 3 * it + 3)
                        b, w, x = 2, gcur[s][:, :], gdT[:, :]
                    at = (4 * s + b) * 512
                    pe.matmul(psf[:, at:at + 512], w, x[:, 0:512], start=True, stop=True)
                    pe.matmul(psf[:, at + 512:at + T], w, x[:, 512:T], start=True, stop=True).then_inc(pe_e[s], 1)
            for s in range(2):
                pe.wait_ge(rwo_done, 2 * it + s + 1)
        phase_over(pe, 4)
        pe.wait_ge(b_lo, 8)
        with pe.Fori(0, 2) as i:
            for s in range(2):
                b = 2 * i + s + BLK_BR
                for j in range(2):
                    if j == 0:
                        pe.wait_ge(lo_done, b + 1)
                        pe.wait_ge(hi_done, b + 1)
                    pe.wait_ge(tile_evac, 2 * b + j + 1)
                    dense_tile(s, j, range(4), bhi[0:4], blo[0:4], out_halves(4 * j), 256)
                    dense_tile(s, j, range(4, 8), bhi[4:8], blo[4:8], out_halves(4 * j + 2), 256).then_inc(tile_done, 1)
        pe.wait_ge(m_lo, KD)
        with pe.Fori(0, 2) as i:
            for s in range(2):
                dense_block(2 * i + s + BLK_OUT, s, mhi, mlo)
        phase_over(pe, 5)
        sum_squares(1)
        pe.wait_ge(h_done, 2 * KD)
        with pe.Fori(0, FF // 2) as i:
            for s in range(2):
                dense_block(2 * i + s + BLK_UP, s, h2hi, h2lo)
        pe.wait_ge(tile_evac, 2 * NBLK + 2)

        def down_unit(n, s, k):
            pe.wait_ge(d_hi, n + 1)
            pe.wait_ge(d_lo, n + 1)
            for f in range(4):
                hi, lo = whi[s][:, f * P:f * P + P], wlo[s][:, f * P:f * P + P]
                outs = out_halves(2 * f, TP - 2)
                for q, (w, x) in enumerate(((hi, dlo[s]), (lo, dhi[s]), (hi, dhi[s]))):
                    for o, v in zip(outs, halves(x, TP - 2)):
                        mm = pe.matmul(o, w, v, start=(k == 0 and q == 0), stop=(k == FF - 1 and q == 2))
            mm.then_inc(d_used, 1)

        for g in range(2):
            if g:
                pe.wait_ge(d_evac, 4)
            for k in range(2):
                down_unit(FF * g + k, k, k)
            with pe.Fori(1, FF // 2 - 1) as i:
                for s in range(2):
                    down_unit(2 * i + s + FF * g, s, 2)
            for k in range(FF - 2, FF):
                down_unit(FF * g + k, k % 2, k)
        pe.wait_ge(d_evac, 8)
        sum_squares(2)

    @block.scalar
    def _(ac):
        st = Steps(ac, act)

        def squares(n, src):
            for k in range(KD):
                if n == 0 and k == 0:
                    ac.wait_ge(x_ld, 16)
                if n == 1:
                    ac.wait_ge(tile_evac, 2 * BLK_OUT + k + 3)
                if n == 2:
                    ac.wait_ge(d_evac, k + 1)
                if k >= 2:
                    ac.wait_ge(sqs_done, n * KD + k - 1)
                ac.activation(sqf[k % 2][:, :], src[:, k, :], ACT.Square).then_inc(sq_done, 1)
            if n == 1:
                next_hi(BLK_UP, 0)
            ac.wait_ge(sq_used, (n + 1) * KD)
            st.last(ac.activation(rs[:, :], tile(4), ACT.Ln, scale=1.0 / D, bias=EPS))
            ac.activation(rs[:, :], rs[:, :], ACT.Exp, scale=-0.5).then_inc(rs_done, 1)

        def modulate(n, scale, shift_at, hi):
            for k in range(KD):
                ac.wait_ge(xr_done, n * KD + k + 1)
                if k >= 2:
                    ac.wait_ge(h_done, n * KD + k - 1)
                for c, (a, w) in enumerate(((L0, LAT), (C0, CTX))):
                    ins = ac.activation(hf[k % 2][:, a:a + w], xr[k % 2][:, a:a + w], ACT.Identity,
                                        scale=scale[:, k, c:c + 1], bias=modT[:, shift_at + k, c:c + 1])
                ins.then_inc(hf_done, 1)
                ac.wait_ge(hf_done, n * KD + k + 1)
                ac.activation(hi[k][:, :], hf[k % 2][:, :], ACT.Copy).then_inc(hh_done, 1)

        def split_hi(b, s):
            ac.activation(whi[s][:, :], raw[s][:, :], ACT.Copy).then_inc(hi_done, 1)

        def next_hi(b, s):
            ac.wait_ge(tile_done, 2 * b - 2)
            ac.wait_ge(w_ld[s], 8 * (b - s) + 16)
            split_hi(b, s)

        ac.wait_ge(par_ld, 16)
        ac.activation(silu_c[:, :, :].rearrange("p k c -> p (k c)"), pc("c", 0, 16), ACT.Tanh, scale=0.5).then_inc(ctanh_done, 1)
        squares(0, xT)
        ac.nop().then_inc(row_done, 2)
        for n in range(ADA_EARLY):
            ac.wait_ge(ada_done, n + 1)
            ac.activation(modrow[0:2, n * 512:n * 512 + 512], bank(2 + n % 2)[0:2], ACT.Copy).then_inc(row_done, 1)
        ac.wait_ge(mod_done, 1)
        modulate(0, sc1g, 0, hhi)
        phase_over(ac, 1)
        ac.nop().then_inc(tile_evac, 2)
        for s in range(2):
            ac.wait_ge(w_ld[s], 16)
            split_hi(s, s)

        def conv_evac(n, j, wcol, fr, fa, conv_k):
            ac.wait_ge(tile_done, n + 1)
            if conv_k is not None:
                ac.wait_ge(conv_done, conv_k)
            ac.activation(fr[j][:, :], tile(2 * j), ACT.Copy)
            ac.activation(fa[j][:, :], tile(2 * j), ACT.Identity, scale=wcol).then_inc(tile_evac, 1)

        for n in range(2):
            conv_evac(n, n, pc("rconv", 3 * n + 1), craw, cacc, None)
        with ac.Fori(0, 3) as i:
            for s in range(2):
                next_hi(2 * i + 2 + s, s)
                for j in range(2):
                    n = 4 * i + 2 + 2 * s + j
                    conv_evac(n, j, pc("rconv", 3 * n + 1), craw, cacc, n - 1)
        for k in range(6):
            b = NBLK_U + k // 2
            if k % 2 == 0:
                next_hi(b + 1, (b + 1) % 2)
            ac.wait_ge(tile_done, 2 * NBLK_U + k + 1)
            ac.activation(qkv[:, k, :], tile(2 * (k % 2)), ACT.Copy).then_inc(tile_evac, 1)
        for b in range(NBLK_U + NBLK_Q, BLK_BR):
            if b + 1 < BLK_BR:
                next_hi(b + 1, (b + 1) % 2)
            for j in range(2):
                f = b - NBLK_U - NBLK_Q
                ac.wait_ge(tile_done, 2 * b + j + 1)
                if f >= 1:
                    ac.wait_ge(g_st[j], 16 * f)
                ac.activation(gout[j][:, :], tile(2 * j), ACT.Tanh, scale=0.5).then_inc(tile_evac, 1)
        phase_over(ac, 2)
        for j in range(5):
            if j >= 2:
                ac.wait_ge(ass_done, j - 1)
            ac.activation(asq[j % 2][:, :], qkv[:, j, :], ACT.Square).then_inc(asq_done, 1)
            ac.wait_ge(ass_done, j + 1)
            if j >= 2:
                ac.wait_ge(aqn_done, j - 1)
            at = 1024 * (j % 2)
            st.last(ac.activation(arn[j % 2][:, :], psf[:, at:at + TP], ACT.Ln, scale=1.0 / 64, bias=EPS))
            ac.activation(arn[j % 2][:, :], arn[j % 2][:, :], ACT.Exp, scale=-0.5).then_inc(arn_done, 1)
        ac.wait_ge(vt_done, 1)
        ac.activation(vt[:, 0:4, :], bank(6).rearrange("p (t n) -> p t n", t=4), ACT.Copy)
        ac.activation(vt[:, 6, :], bank(7, P), ACT.Copy).then_inc(vt_copied, 1)

        def head_out(h):
            rows = slice(64 * (h % 2), 64 * (h % 2) + 64)
            ac.wait_ge(o_done, h + 1)
            ac.activation(aT[rows, h // 2, L0:L0 + LAT], bank(6 + h % 2)[rows], ACT.Copy).then_inc(o_copied, 1)

        def turned_half(n):
            ac.wait_ge(pt_done, n + 1)
            if n >= 8:
                ac.wait_ge(o_done, n // 4 - 1)
            ac.activation(pt[n // 4 % 2][:, 3:6, n % 4 * P:n % 4 * P + P], bank(5, 3 * P).rearrange("p (c n) -> p c n", c=3),
                          ACT.Copy).then_inc(pt_copied_a, 1)

        for n in range(32):
            ac.wait_ge(max_done, n + 1)
            if n >= 2:
                ac.wait_ge(pt_done, n - 1)
            ac.activation(pr[n % 2][:, :], psf[:, 1024 * (n % 2):1024 * (n % 2) + 768], ACT.Exp,
                          bias=nmax[:, n:n + 1], accum_out=lsum[:, n:n + 1]).then_inc(exp_done, 1)
            if n:
                turned_half(n - 1)
            if n % 4 == 1 and n > 4:
                head_out(n // 4 - 1)
        turned_half(31)
        head_out(7)
        for g in range(2):
            ac.wait_ge(max_done, 33 + g)
            for j in range(4):
                m = 32 + 4 * g + j
                ins = ac.activation(prc[:, g, j, :], bank(2 * g + j % 2, P, P * (j // 2)), ACT.Exp, bias=nmax[:, m:m + 1],
                                    accum_out=lsum[:, m:m + 1])
            ins.then_inc(exp_done, 1)
        for g in range(2):
            ac.wait_ge(o_done, 9 + g)
            ac.activation(aT[:, 2 * g:2 * g + 2, C0:C0 + CTX], bank(6 + g, 2 * P).rearrange("p (k n) -> p k n", k=2),
                          ACT.Copy).then_inc(o_copied, 1)
        phase_over(ac, 3)
        def ada_row(it, m):
            n = 4 * it + ADA_EARLY + m
            ac.wait_ge(ada_done, n + 1)
            ac.wait_ge(modt_done, n - 2)
            ac.activation(adrow[m % 2][:, :], bank(4 + m % 2)[0:2], ACT.Copy).then_inc(row_done, 1)

        ac.activation(wdad[0:64, :], wdad[0:64, :], ACT.Tanh)
        ac.activation(gdT[:, :], gdT[:, :], ACT.Tanh, scale=0.5).then_inc(low_done, 1)
        ac.nop().then_inc(prep_read, 2)
        with ac.Fori(0, 2) as it:
            for s in range(2):
                ac.wait_ge(rw_ld[s], 32 * it + 32)
                ac.activation(tb[11 * s][:, :], uc[s][:, 1, :], ACT.Square, scale=pc("kk", 2 * it + s)).then_inc(ac_prep, 1)
            for s in range(2):
                ac.wait_ge(pe_prep, 10 * it + s + 1)
                ac.activation(rn[s][:, :], psf[:, 1024 * s:1024 * s + T], ACT.Ln, bias=1e-12).then_inc(prep_read, 1)
            for s in range(2):
                ac.wait_ge(prep_read, 10 * it + s + 3)
                ac.activation(rn[s][:, :], rn[s][:, :], ACT.Exp, scale=-0.5).then_inc(ac_prep, 1)
            for s in range(2):
                if s == 1:
                    ac.wait_ge(dv_prep, 10 * it + 5)
                    ada_row(it, 0)
                for d in range(2):
                    if d == 1:
                        ac.wait_ge(dv_prep, 10 * it + 5 * s + 3)
                    for j, (dst, bias) in enumerate(((tb[3], hw0), (tb[4], ha0))):
                        n = 2 + 4 * s + 2 * d + j
                        at = 1024 * (n % 2)
                        ac.wait_ge(pe_prep, 10 * it + n + 1)
                        ac.activation(dst[:, :], psf[:, at:at + T], ACT.Tanh, scale=0.5,
                                      bias=bias[:, 2 * it + s, d:d + 1]).then_inc(prep_read, 1)
                    ac.wait_ge(dv_prep, 10 * it + 5 * s + 1)
                    ac.wait_ge(prep_read, 10 * it + 4 * s + 6 + 2 * d)
                    ac.activation(tb[0][:, :], tb[4][:, :], ACT.Identity, scale=kfc[s][:, 0:1], bias=kfc[s][:, 1:2])\
                        .then_inc(kf_done, 1)
                    ac.wait_ge(dv_prep, 10 * it + 5 * s + 2 + 2 * d)
                    ac.wait_ge(pl_prep, 4 * it + 2 * s + d + 1)
                    ci, cx = tb[6], tb[7]
                    if s == 1 and d == 1:
                        ada_row(it, 1)
                    for dst, src, sg in ((tb[8], cx, 1.0), (tb[9], ci, 1.0), (tb[10], ci, -1.0)) if d == 0 else \
                            ((tb[8], ci, -1.0), (tb[9], cx, -1.0), (tb[10], cx, 1.0)):
                        ins = ac.activation(dst[:, :], src[:, :], ACT.Exp, scale=sg)
                    ins.then_inc(ac_prep, 1)
                    for n, src in ((d, by_tile(tb[5][:, :])[:, :, 63]), (1 - d, ecin[s][:, d, :]),
                                   (2, by_tile(tb[5][:, :])[:, :, P - 1])):
                        ac.activation(ecol[s][:, n, d, :], src, ACT.Exp)
            for m in range(2, 4):
                ada_row(it, m)
            for t, name, s in in_order(AC_ST):
                b = 4 * s
                ac.wait_ge(pe_g[s], at_stage(PE_ST, it, t, name.replace("E", "H")))
                if name == "TR":
                    src = bank(b + 1, 2 * P).rearrange("p (d h n) -> p d h n", d=2, h=2)
                    for d in range(2):
                        ac.activation(xa[s][:, d, 0:4:3, :], src[:, d], ACT.Copy)
                    ac.activation(vz[s][:, 1:3, :], bank(b + 1, P, 2 * P).rearrange("p (h n) -> p h n", h=2), ACT.Copy)
                    ins = ac.activation(bkt[s][:, :, :, :].rearrange("p d n c -> p (d n c)"), bank(b + 2), ACT.Copy)
                elif name == "X0":
                    ins = ac.activation(xa[s][:, :, 1:3, :], own_columns(b + 3), ACT.Copy)
                elif name in ("WU",) or name[0] == "E":
                    ins = ac.activation(hm[s][:, :, :, :].rearrange("p d h n -> p (d h n)"), bank(b), ACT.Copy)
                elif name == "QY":
                    src = [bank(b + 1 + 2 * h, 2 * P).rearrange("p (d n) -> p d n", d=2) for h in range(2)]
                    ac.activation(qy[s][0:64, t, :, 1, :], src[1][0:64], ACT.Copy)
                    ins = ac.activation(qy[s][64:128, t, :, 0, :], src[0][64:128], ACT.Copy)
                else:
                    ins = ac.activation(mn[s][:, t, :, :].rearrange("p (d h) c -> p d h c", d=2), own_columns(b + 2), ACT.Copy)
                ins.then_inc(ac_g[s], 1)
            for s in range(2):
                at = (4 * s + 2) * 512
                ac.wait_ge(pe_e[s], 5 * it + 1)
                ac.activation(ep[s][0][:, :], psf[:, at:at + T], ACT.Copy).then_inc(ac_e[s], 1)
            for s in range(2):
                ac.wait_ge(dv_e[s], 2 * it + 1)
                ac.activation(ep[s][2][:, :], ep[s][1][:, :], ACT.Square).then_inc(ac_e[s], 1)
            for s in range(2):
                at = (4 * s + 2) * 512
                ac.wait_ge(pe_e[s], 5 * it + 3)
                ac.activation(ep[s][2][:, :], psf[:, at:at + T], ACT.Ln, scale=1.0 / 64, bias=GN_EPS).then_inc(ln_done, 1)
                ac.wait_ge(ln_done, 2 * it + s + 1)
                ac.activation(ep[s][2][:, :], ep[s][2][:, :], ACT.Exp, scale=-0.5).then_inc(ac_e[s], 1)
            for s in range(2):
                ac.wait_ge(rwo_done, 2 * it + s + 1)
        phase_over(ac, 4)
        for b in range(BLK_BR, BLK_BR + 2):
            ac.wait_ge(w_ld[b % 2], 8 * (b - b % 2) + 16)
            split_hi(b, b % 2)
        for k in range(8):
            ac.wait_ge(b_ld[k], 16)
            ac.activation(bhi[k][:, :], bld[k][:, :], ACT.Copy).then_inc(b_hi, 1)
        for f in range(KD):
            if f % 2 == 1:
                b = BLK_BR + 2 + f // 2
                if b < BLK_UP:
                    next_hi(b, b % 2)
            ac.wait_ge(mf_done, f + 1)
            ac.activation(mhi[f][:, :], m1[f % 2][:, :], ACT.Copy).then_inc(m_hi, 1)
        for b in range(BLK_OUT + 2, BLK_UP):
            next_hi(b, b % 2)
        phase_over(ac, 5)
        squares(1, x1)
        modulate(1, sc2g, 24, h2hi)
        next_hi(BLK_UP + 1, 1)

        def up_block(b, j0, s, first, split):
            for j in range(2):
                conv_evac(2 * b + j, j, pc("fconv", 6 * j0 + 3 * j + 1), fraw, facc, None if first else 2 * j0 + NU + j - 1)
            if split:
                next_hi(b + 2, s)
            ac.wait_ge(conv_done, 2 * j0 + NU + 2)
            ac.activation(ftg[:, :], fcg[:, :], ACT.Tanh, scale=0.5).then_inc(tg_done, 1)

        for j0 in range(2):
            up_block(BLK_UP + j0, j0, j0 % 2, j0 == 0, True)
        with ac.Fori(1, FF // 2 - 1) as i:
            for s in range(2):
                up_block(2 * i + s + BLK_UP, 2 * i + s, s, False, True)
        for j0 in range(FF - 2, FF):
            up_block(BLK_UP + j0, j0, j0 % 2, False, False)

        def down_hi(n, s, k, first):
            ac.wait_ge(wd_ld[s], 8 * (n - s) + 16)
            if not first:
                ac.wait_ge(d_used, n - 1)
            ac.activation(whi[s][:, 0:512], raw[s][:, 0:512], ACT.Copy)
            ac.activation(dhi[s][:, :], af[:, k, :], ACT.Copy).then_inc(d_hi, 1)

        ac.wait_ge(act_done, FF)
        ac.wait_ge(tile_done, 2 * NBLK)
        for k in range(2):
            down_hi(k, k, k, True)
        for g in range(2):
            with ac.Fori(1 - g, FF // 2) as i:
                for s in range(2):
                    down_hi(2 * i + s + FF * g, s, 2 * i + s, False)
        squares(2, x1)

    @block.vector
    def _(dv):
        st = Steps(dv, dve)
        TT, STT, TS = dv.tensor_tensor, dv.scalar_tensor_tensor, dv.tensor_scalar

        def split_squares(n):
            for k in range(KD):
                dv.wait_ge(sq_done, n * KD + k + 1)
                if k >= 2:
                    dv.wait_ge(sq_used, n * KD + k - 1)
                st.last(dv.tensor_copy(sqh[k % 2][:, :], sqf[k % 2][:, :]))
                TT(sql[k % 2][:, :], sqf[k % 2][:, :], sqh[k % 2][:, :].bitcast(F32), ALU.subtract).then_inc(sqs_done, 1)

        def modulate(n, src, hi, lo):
            dv.wait_ge(rs_done, n + 1)
            for k in range(KD + 1):
                if k < KD:
                    if k >= 2:
                        dv.wait_ge(hf_done, n * KD + k - 1)
                    TT(xr[k % 2][:, :], src[:, k, :], rs[:, :], ALU.mult).then_inc(xr_done, 1)
                if k:
                    dv.wait_ge(hh_done, n * KD + k)
                    TT(lo[k - 1][:, :], hf[(k - 1) % 2][:, :], hi[k - 1][:, :].bitcast(F32), ALU.subtract).then_inc(h_done, 1)

        def next_lo(b, s):
            dv.wait_ge(hi_done, b + 1)
            TT(wlo[s][:, :], raw[s][:, :], whi[s][:, :].bitcast(F32), ALU.subtract).then_inc(lo_done, 1)

        def borders(t):
            for a, n in ((0, 1), (L0 + LAT, 1), (C0 + CTX, 2)):
                dv.memset(t[:, a:a + n], 0.0)

        dv.memset(onesr[:, :].bitcast(F32), 1.0).then_inc(setup_done, 1)
        dv.wait_ge(par_ld, 16)
        dv.wait_ge(ctanh_done, 1)
        sc, cin = silu_c[:, :, :].rearrange("p k c -> p (k c)"), pc("c", 0, 16)
        st.last(STT(sc, sc, 1.0, cin, ALU.add, ALU.mult))
        TS(sc, sc, 0.5, None, ALU.mult).then_inc(silu_done, 1)
        TS(hw0[:, :, :].rearrange("p k c -> p (k c)"), pc("w0", 0, 8), 0.5, None, ALU.mult)
        TS(ha0[:, :, :].rearrange("p k c -> p (k c)"), pc("a0", 0, 8), 0.5, None, ALU.mult)
        TS(kac[:, 0, :], pc("ka", 0, 4), 0.5, None, ALU.mult)
        TS(kac[:, 1, :], pc("ka", 0, 4), -0.5, 1.0, ALU.mult, ALU.add)
        TS(qg8[:, :], pc("qg"), 0.125, None, ALU.mult)
        for s in range(2):
            dv.memset(hf[s][:, :], 0.0)
        split_squares(0)
        def mod_columns(at):
            return TT(modT[:, ds(at, 16), :], bank(6, 32).rearrange("p (k c) -> p k c", c=2),
                      pc("bada", at, 16).unsqueeze(2).broadcast_to([P, 16, 2]), ALU.add)

        def one_plus(dst, at, g):
            return STT(dst[:, :, :], modT[:, at:at + KD, :], 1.0, pc(g, 0, KD).unsqueeze(2).broadcast_to([P, KD, 2]),
                       ALU.add, ALU.mult)

        dv.wait_ge(modt_done, ADA_EARLY - 1)
        st.last(mod_columns(0))
        one_plus(sc1g, 8, "g1").then_inc(mod_done, 1)
        modulate(0, xT, hhi, hlo)
        phase_over(dv, 1)
        next_lo(0, 0)
        next_lo(1, 1)

        def convolve(n, j, taps, fr, fa, outs):
            dv.wait_ge(tile_evac, n + 3)
            st.last(STT(fa[j][:, 1:TP - 1], fr[j][:, 0:TP - 2], taps(0), fa[j][:, 1:TP - 1], ALU.mult, ALU.add))
            for a, w, o in outs:
                ins = STT(o, fr[j][:, a + 1:a + 1 + w], taps(2), fa[j][:, a:a + w], ALU.mult, ALU.add)
            ins.then_inc(conv_done, 1)

        def u_tile(n, j, dst, wait_stored):
            if wait_stored is not None:
                dv.wait_ge(u_st[j], wait_stored)
            convolve(n, j, lambda q: pc("rconv", 3 * n + q), craw, cacc,
                     ((L0, LAT, dst[:, 0:LAT]), (C0, CTX, dst[:, LAT:T])))

        for n in range(2):
            u_tile(n, n, uout[n], None)
        with dv.Fori(0, 2) as i:
            st.enter(i, 4)
            for s in range(2):
                next_lo(2 * i + 2 + s, s)
                for j in range(2):
                    u_tile(4 * i + 2 + 2 * s + j, j, uout[j], 32 * i + 16 + 16 * s)
            st.leave(2)
        next_lo(6, 0)
        for j in range(2):
            u_tile(10 + j, j, uout[j], 80)
        next_lo(7, 1)
        u_tile(12, 0, wdad, None)
        u_tile(13, 1, gdT, None)
        with dv.Fori(4, BLK_BR // 2) as i:
            for s in range(2):
                next_lo(2 * i + s, s)
        phase_over(dv, 2)
        for k in range(4):
            borders(aT[:, k, :])
        for j in range(5):
            dv.wait_ge(arn_done, j + 1)
            STT(qkv[:, j, :], qkv[:, j, :], qg8[:, :] if j < 4 else pc("kg"), arn[j % 2][:, :], ALU.mult, ALU.mult)\
                .then_inc(aqn_done, 1)
            dv.wait_ge(aqn_done, j + 1)
            if j == 4:
                for kv in range(2):
                    for h in range(2):
                        dv.tensor_copy(k2c[64 * h:64 * h + 64, kv, :], qkv[64 * kv:64 * kv + 64, 4, C0:C0 + CTX])
            row = qkv[:, j, L0:L0 + LAT]
            TT(rt1[:, :], row, cosT, ALU.mult)
            dv.wait_ge(arot_done, j + 1)
            st.last(TT(rt2[:, :], bank(4 + j % 2), sinT, ALU.mult))
            if j < 4:
                TT(row, rt1[:, :], rt2[:, :], ALU.add).then_inc(aq_done, 1)
                dv.wait_ge(aq_done, j + 1)
                for h in range(2):
                    half = qkv[64 * h:64 * h + 64, j, L0:L0 + LAT]
                    ins = dv.tensor_copy(qst[h][0:64, j, :], half)
                st.last(ins)
                for h in range(2):
                    half = qkv[64 * h:64 * h + 64, j, L0:L0 + LAT]
                    ins = TT(qst[h][64:128, j, :], half, qst[h][0:64, j, :].bitcast(F32), ALU.subtract)
                ins.then_inc(qst_done, 1)
            else:
                for kv in range(2):
                    rows = slice(64 * kv, 64 * kv + 64)
                    ins = TT(k2[:, kv, 0:LAT], rt1[rows, :], rt2[rows, :], ALU.add)
                dv.wait_ge(cache_ld, 48)
                st.last(ins)
                for h in range(2):
                    ins = dv.tensor_copy(kst[64 * h:64 * h + 64, 0], k2[:, :, :])
                st.last(ins)
                for h in range(2):
                    ins = TT(kst[64 * h:64 * h + 64, 1], k2[:, :, :], kst[0:64, 0].bitcast(F32), ALU.subtract)
                ins.then_inc(qst_done, 1)

        def score_max(n):
            dv.wait_ge(s_done, n + 1)
            dv.tensor_reduce(nmax[:, n:n + 1], psf[:, 1024 * (n % 2):1024 * (n % 2) + 768], AX, ALU.max, negate=True)\
                .then_inc(max_done, 1)

        score_max(0)
        for n in range(32):
            h, qt = n // 4, n % 4
            dv.wait_ge(exp_done, n + 1)
            st.last(dv.reciprocal(rsum[:, n:n + 1], lsum[:, n:n + 1]))
            if n >= 2:
                dv.wait_ge(pt_done, n - 1)
            TS(rdiag[n % 2][:, :], ident, rsum[:, n:n + 1], None, ALU.mult).then_inc(prob_done, 1)
            if n < 31:
                score_max(n + 1)
            dv.wait_ge(pt_done, n + 1)
            if h >= 2:
                dv.wait_ge(o_done, h - 1)
            dv.tensor_copy(pt[h % 2][:, 0:3, qt * P:qt * P + P], bank(4, 3 * P).rearrange("p (c n) -> p c n", c=3))\
                .then_inc(pt_copied, 1)
        for g in range(2):
            dv.wait_ge(s_done, 33 + g)
            for r in range(2):
                ins = dv.tensor_reduce(nmax[:, 32 + 4 * g + r:36 + 4 * g:2], bank(2 * g + r, 2 * P).rearrange("p (h n) -> p h n", h=2),
                                       AX, ALU.max, negate=True)
            ins.then_inc(max_done, 1)
        for g in range(2):
            dv.wait_ge(exp_done, 33 + g)
            r = rsum[:, 32 + 4 * g:36 + 4 * g]
            st.last(dv.reciprocal(r, lsum[:, 32 + 4 * g:36 + 4 * g]))
            TT(prc[:, g], prc[:, g], r.unsqueeze(2).broadcast_to([P, 4, P]), ALU.mult).then_inc(prob_done, 1)
            dv.wait_ge(pt_done, 33 + g)
            dv.tensor_copy(ptc[:, g], bank(4 + g).rearrange("p (h n) -> p h n", h=4)).then_inc(pt_copied, 1)
        phase_over(dv, 3)
        dv.wait_ge(low_done, 1)
        TS(gdT[:, :], gdT[:, :], 0.5, 0.5, ALU.mult, ALU.add)
        for s in range(2):
            dv.memset(vz[s][:, 0, :], 0.0)
            dv.memset(vz[s][:, 3, :], 0.0)

        def prepare(it, s):
            hp = 2 * it + s
            uk = uc[s][:, 1, :]
            kk, lw, rate, ci, cim, cxm = (tb[2], rn[1])[s], tb[3], tb[4], tb[5], tb[6], tb[7]
            dv.tensor_copy(kfc[s][:, :], kac[:, :, ds(hp, 1)].rearrange("p a b -> p (a b)"))
            dv.wait_ge(ac_prep, 8 * it + s + 3)
            STT(kk[:, :], uk, pc("kk", hp), rn[s][:, :], ALU.mult, ALU.mult).then_inc(dv_prep, 1)
            for d in range(2):
                dv.wait_ge(prep_read, 10 * it + 4 * s + 6 + 2 * d)
                st.last(TS(lw[:, :], lw[:, :], -EHALF, -EHALF, ALU.mult, ALU.add))
                st.last(dv.tensor_tensor_scan(ci[:, :], reset, lw[:, :], 0.0, ALU.mult, ALU.add))
                mid, end = by_tile(ci[:, :])[:, :, 63], by_tile(ci[:, :])[:, :, P - 1]
                TT(ecin[s][:, d, :], end, mid, ALU.subtract)
                st.last(TT(by_tile(cim[:, :]), by_tile(ci[:, :]), mid.unsqueeze(2).broadcast_to([P, NT, P]), ALU.subtract))
                TT(cxm[:, :], cim[:, :], lw[:, :], ALU.subtract).then_inc(dv_prep, 1)
                kd = ksum[s] if d == 0 else tb[0]
                dv.wait_ge(kf_done, 4 * it + 2 * s + d + 1)
                m_kd = st.do(TT(kd[:, :], tb[0][:, :], uk, ALU.mult))
                if d == 0:
                    dv.wait_ge(dv_prep, 10 * it + 5 * s + 1)
                m_b = st.do(STT(tb[1][:, :], rate[:, :], 1.0, kk[:, :], ALU.add, ALU.mult))
                st.need(m_kd)
                if d == 1:
                    TT(ksum[s][:, :], ksum[s][:, :], kd[:, :], ALU.add)
                dv.wait_ge(ac_prep, 8 * it + 2 * s + 5 + d)
                ea, eb = tb[8], tb[10]
                for h in range(2):
                    rows = slice(64 * h, 64 * h + 64)
                    STT(ar[s][rows, d, :, h, 0, :], by_tile(kk[rows, :]), -1.0, by_tile(ea[rows, :]), ALU.mult, ALU.mult)
                st.need(m_b)
                TT(kt[s][:, d, :], kd[:, :], eb[:, :], ALU.mult)
                STT(bt[s][:, d, :], tb[1][:, :], 0.5, eb[:, :], ALU.mult, ALU.mult).then_inc(dv_prep, 1)

        def chunk_stage(it, t, s, name):
            b = 4 * s
            need = {"AK": "KAB", "AB": "KAB", "R0": None, "QY": "QY"}.get(name, None)
            if name[0] in "UV":
                need = "G" + name[1]
            if need:
                dv.wait_ge(pe_g[s], at_stage(PE_ST, it, t, need))
            if name in ("AK", "AB"):
                dst, o = (akm, 0) if name == "AK" else (abm, 2)
                for h in range(2):
                    ins = TT(dst[s][:, :, h].rearrange("p d a n -> p d (a n)"), bank(b + o + h).rearrange("p (d n) -> p d n", d=2),
                             mar.rearrange("p d a n -> p d (a n)"), ALU.mult)
            elif name == "R0":
                dv.wait_ge(dv_g[s], at_stage(DV_ST, it, t, "AB"))
                st.last(TT(rm[s][:, :, :, :], abm[s][:, :, :, 0, :], m1t.unsqueeze(2).broadcast_to([P, 2, 2, P]), ALU.mult))
                r4 = rm[s][:, :, :, :].rearrange("p d h n -> p (d h) n")
                st.last(TT(r4, r4, ident.unsqueeze(1).broadcast_to([P, 4, P]), ALU.add))
                ins = dv.transpose(tm[s][:, :, :, :].rearrange("p d h n -> p (d h n)"), rm[s][:, :, :, :].rearrange("p d h n -> p (d h n)"))
            elif name[0] in "UV":
                l = int(name[1])
                t1, r1 = (x[s][:, :, :, :].rearrange("p d h n -> p (d h n)") for x in (tm, rm))
                if name[0] == "U":
                    dv.wait_ge(dv_g[s], at_stage(DV_ST, it, t, "R0" if l == 0 else f"V{l - 1}"))
                    ins = TT(t1, bank(b + 1), t1, ALU.add)
                elif l < NL - 2:
                    dv.wait_ge(dv_g[s], at_stage(DV_ST, it, t, f"U{l}"))
                    ins = dv.transpose(r1, t1)
                else:
                    ins = TT(r1, bank(b + 2), r1, ALU.add)
            else:
                for h in range(2):
                    rows = slice(64 * h, 64 * h + 64)
                    src = bank(b + 1 + 2 * h, 2 * P).rearrange("p (d n) -> p d n", d=2)
                    ins = TT(qy[s][rows, t, :, h, :], src[rows], ar[s][rows, :, t, h, 1, :], ALU.add)
            ins.then_inc(dv_g[s], 1)

        def states(it):
            for s in range(2):
                dv.wait_ge(pe_s, 8 * it + s + 1)
                for d in range(2):
                    ins = TS(stf[s][:, d, :], bank(4 * s + 3, 64, 64 * d), ecol[s][:, 1, d, 4:5], None, ALU.mult)
                ins.then_inc(dv_s, 1)
            for j in range(4):
                for s in range(2):
                    src, new = stv[s] if j == 0 else stx[s][:, (j - 1) % 2], stx[s][:, j % 2]
                    for d in range(2):
                        t = j if d == 0 else 3 - j
                        for h in range(2):
                            rows = slice(64 * h, 64 * h + 64)
                            ins = TS(si[s][rows, t, d, h, :], src[rows, d, :], ecol[s][rows, 0, d, t:t + 1], None, ALU.mult)
                    ins.then_inc(dv_s, 1)
                    if j < 3:
                        for d in range(2):
                            t = j if d == 0 else 3 - j
                            ins = TS(new[:, d, :], src[:, d, :], ecol[s][:, 2, d, t:t + 1], None, ALU.mult)
                        kept = st.do(ins)
                if j < 3:
                    st.need(kept)
                    for s in range(2):
                        dv.wait_ge(pe_s, 8 * it + 2 + 2 * j + s + 1)
                        for d in range(2):
                            t = j if d == 0 else 3 - j
                            new = stx[s][:, j % 2, d, :]
                            ins = STT(new, bank(4 * s, 64, 64 * d), ecol[s][:, 1, d, t:t + 1], new,
                                      ALU.mult, ALU.add)
                        kept = st.do(ins)
                    st.need(kept)

        def epilogue(it):
            for s in range(2):
                at = 4 * s * 512
                dv.wait_ge(pe_e[s], 5 * it + 2)
                STT(ep[s][1][:, :], psf[:, at:at + T], -1.0 / 64, ep[s][0][:, :], ALU.mult, ALU.add).then_inc(dv_e[s], 1)
                STT(ep[s][3][:, :], uc[s][:, 0, :], pc("rk", 2 * it + s), ksum[s][:, :], ALU.mult, ALU.mult)\
                    .then_inc(dv_e[s], 1)
            for s in range(2):
                at = 4 * s * 512
                y, e3 = ep[s][1][:, :], ep[s][3][:, :]
                dv.wait_ge(ac_e[s], 3 * it + 3)
                st.last(TT(y, y, ep[s][2][:, :], ALU.mult))
                st.last(TS(y, y, pc("lng", 2 * it + s), pc("lnb", 2 * it + s), ALU.mult, ALU.add))
                dv.wait_ge(pe_e[s], 5 * it + 4)
                st.last(TT(e3, psf[:, at:at + T], uc[s][:, 2, :], ALU.mult))
                st.last(TT(y, y, e3, ALU.add))
                borders(rwo[s])
                dv.wait_ge(pe_e[s], 5 * it + 5)
                for a, w, c in ((0, LAT, L0), (LAT, CTX, C0)):
                    ins = TT(rwo[s][:, c:c + w], psf[:, at + 1024 + a:at + 1024 + a + w], y[:, a:a + w], ALU.mult)
                ins.then_inc(rwo_done, 1)

        with dv.Fori(0, 2) as it:
            st.enter(it, STEPS_RWKV)
            for s in range(2):
                prepare(it, s)
            dv.wait_ge(modt_done, 4 * it + ADA_EARLY + 3)
            mod_columns(16 * it + 16).then_inc(mod_done, 1)
            for t, name, s in in_order(DV_ST):
                chunk_stage(it, t, s, name)
            states(it)
            epilogue(it)
            st.leave(2)
        dv.wait_ge(mod_done, 3)
        one_plus(sc2g, 32, "g2")
        TS(g1h[:, :, :], modT[:, 16:16 + KD, :], 0.5, None, ALU.mult)
        TS(g2h[:, :, :], modT[:, 40:40 + KD, :], 0.5, None, ALU.mult)
        phase_over(dv, 4)
        for b in range(BLK_BR, BLK_BR + 2):
            next_lo(b, b % 2)
        for k in range(8):
            dv.wait_ge(b_hi, k + 1)
            TT(blo[k][:, :], bld[k][:, :], bhi[k][:, :].bitcast(F32), ALU.subtract).then_inc(b_lo, 1)

        def merged_lo(f):
            dv.wait_ge(m_hi, f + 1)
            TT(mlo[f][:, :], m1[f % 2][:, :], mhi[f][:, :].bitcast(F32), ALU.subtract).then_inc(m_lo, 1)

        for f in range(KD):
            j = f % 2
            dv.wait_ge(tile_done, 2 * BLK_BR + f + 1)
            dv.wait_ge(gl_ld[j], 16 * (f // 2 + 1))
            if f >= 2:
                dv.wait_ge(m_lo, f - 1)
            STT(m1[j][:, :], gld[j][:, 0, :], 1.0, tile(4 * j), ALU.add, ALU.mult)
            STT(m2[j][:, :], gld[j][:, 1, :], 1.0, tile(4 * j + 2), ALU.add, ALU.mult).then_inc(tile_evac, 1)
            dv.wait_ge(tile_evac, 2 * BLK_BR + f + 3)
            TT(m1[j][:, :], m1[j][:, :], m2[j][:, :], ALU.add).then_inc(mf_done, 1)
            if f % 2 == 1:
                next_lo(BLK_BR + 2 + f // 2, (f // 2) % 2)
            if f:
                merged_lo(f - 1)
        merged_lo(KD - 1)
        dv.wait_ge(x1_ld, 16)
        for o in range(KD):
            dv.wait_ge(tile_done, 2 * BLK_OUT + o + 1)
            for c, (a, w) in enumerate(((L0, LAT), (C0, CTX))):
                ins = STT(x1[:, o, a:a + w], tile(2 * (o % 2))[:, a:a + w], g1h[:, o, c:c + 1], x1[:, o, a:a + w],
                          ALU.mult, ALU.add)
            ins.then_inc(tile_evac, 1)
            if o in (1, 3):
                next_lo(BLK_OUT + 2 + o // 2, (o // 2) % 2)
        phase_over(dv, 5)
        for s in range(2):
            dv.memset(hf[s][:, :], 0.0)
        split_squares(1)
        next_lo(BLK_UP, 0)
        modulate(1, x1, h2hi, h2lo)
        next_lo(BLK_UP + 1, 1)

        def up_block(b, j0, s, split):
            for j, dst in ((0, fcu), (1, fcg)):
                convolve(2 * b + j, j, lambda q, j=j: pc("fconv", 6 * j0 + 3 * j + q), fraw, facc, ((1, TP - 2, dst[:, :]),))
            if split:
                next_lo(b + 2, s)
            dv.wait_ge(tg_done, j0 + 1)
            st.last(STT(fcg[:, :], ftg[:, :], 1.0, fcg[:, :], ALU.add, ALU.mult))
            TT(af[:, j0, :], fcg[:, :], fcu[:, :], ALU.mult).then_inc(act_done, 1)

        for j0 in range(2):
            up_block(BLK_UP + j0, j0, j0 % 2, True)
        with dv.Fori(1, FF // 2 - 1) as i:
            st.enter(i - 1, 6)
            for s in range(2):
                up_block(2 * i + s + BLK_UP, 2 * i + s, s, True)
            st.leave(FF // 2 - 2)
        for j0 in range(FF - 2, FF):
            up_block(BLK_UP + j0, j0, j0 % 2, False)
        for g in range(2):
            with dv.Fori(0, FF // 2) as i:
                for s in range(2):
                    n = 2 * i + s + FF * g
                    dv.wait_ge(d_hi, n + 1)
                    TT(wlo[s][:, 0:512], raw[s][:, 0:512], whi[s][:, 0:512].bitcast(F32), ALU.subtract)
                    TT(dlo[s][:, :], af[:, 2 * i + s, :], dhi[s][:, :].bitcast(F32), ALU.subtract).then_inc(d_lo, 1)
            dv.wait_ge(d_used, FF * (g + 1))
            for f in range(4):
                o = 4 * g + f
                for c, (a, w) in enumerate(((L0, LAT), (C0, CTX))):
                    ins = STT(x1[:, o, a:a + w], tile(2 * f)[:, a - 1:a - 1 + w], g2h[:, o, c:c + 1], x1[:, o, a:a + w],
                              ALU.mult, ALU.add)
                ins.then_inc(d_evac, 1)
        split_squares(2)
        dv.wait_ge(rs_done, 3)
        for k in range(KD):
            if k >= 2:
                dv.wait_ge(y_st[k % 2], 16 * (k // 2))
            STT(yout[k % 2][:, :], x1[:, k, :], pc("gf", k), rs[:, :], ALU.mult, ALU.mult).then_inc(yo_done, 1)

    ctx.close()


def feature_columns(*vectors):
    return np.stack([np.asarray(v).reshape(-1, P).T for v in vectors], -1)


def blocks(w, width):
    rows, cols = w.shape
    return np.ascontiguousarray(w.reshape(rows // P, P, cols // width, width).transpose(2, 1, 0, 3))


def pad_tokens(latent, context):
    out = np.zeros((P, KD, TP), np.float32)
    for a, x in ((L0, latent), (C0, context)):
        out[:, :, a:a + x.shape[0]] = x.reshape(x.shape[0], KD, P).transpose(2, 1, 0)
    return out


def lay_out(i):
    i = {k: np.asarray(v) for k, v in i.items()}
    l = 0
    taps = lambda w: w.reshape(3, -1, P).transpose(2, 1, 0)
    fc = i["ffn_conv"][l].reshape(3, 2, FF, P).transpose(0, 2, 1, 3).reshape(3, -1)
    par = [feature_columns(i["c"][0], i["c_ctx"]), feature_columns(i["b_ada"][l]), feature_columns(i["norm1_g"][l]),
           feature_columns(i["norm2_g"][l]), feature_columns(i["final_norm_g"]),
           np.concatenate([i["q_norm_g"][l]] * 2)[:, None], np.concatenate([i["k_norm_g"][l]] * 2)[:, None],
           taps(i["rwkv_conv"][l]), taps(fc), feature_columns(*i["rwkv_w0"][l]), feature_columns(*i["rwkv_a0"][l]),
           feature_columns(i["rwkv_k_k"][l]), feature_columns(i["rwkv_k_a"][l]), feature_columns(i["rwkv_r_k"][l].reshape(-1)),
           feature_columns(i["rwkv_ln_g"][l]), feature_columns(i["rwkv_ln_b"][l])]
    par = np.ascontiguousarray(np.concatenate([p.reshape(P, -1) for p in par], 1))
    w = i["w_in"][l]
    gates = w[:, 2560:].reshape(D, 2, KD, P).transpose(0, 2, 1, 3).reshape(D, -1)
    w = np.concatenate([w[:, 768:2560], w[:, 0:768], gates], 1)
    up = i["ffn_up"][l].reshape(D, 2, FF, P).transpose(0, 2, 1, 3).reshape(D, -1)
    br = np.concatenate([i["w_attn_br"][l], i["w_rwkv_br"][l]], 0)
    wblk = np.concatenate([blocks(x, 256) for x in (w, br, i["w_out"][l], up)], 0).reshape(NBLK, P, WEL)
    wdn = np.ascontiguousarray(i["ffn_down"][l].reshape(FF, P, 2, 512).transpose(2, 0, 1, 3)).reshape(2 * FF, P, 512)
    low = np.concatenate([i["rwkv_w2"][l], i["rwkv_a2"][l]], 1)
    wlow = low.reshape(2, P, 4, P).transpose(2, 1, 0, 3).reshape(4, P, 2 * P)
    g2w = i["rwkv_g2"][l].reshape(P, 4, P).transpose(1, 0, 2)
    state = i["state_rwkv"][0, l].reshape(2, 4, 2, 64, 64).transpose(1, 2, 4, 0, 3).reshape(4, P, P)
    return {
        "par": par, "con": constants(), "x": pad_tokens(i["x_sample"][0], i["x_prompt"][0]),
        "wada": blocks(i["w_ada"][l], 512), "wblk": wblk, "wdn": wdn,
        "ck": np.ascontiguousarray(i["cache_k"][0, l].transpose(0, 2, 1)),
        "cv": np.ascontiguousarray(i["cache_v"][0, l].reshape(2, 2, P, 64).transpose(2, 1, 0, 3)).reshape(P, 2, P),
        "hpw": np.ascontiguousarray(np.concatenate([wlow, g2w, state], 2)),
    }


OUTS = (("y", (KD, P, TP)), ("nk", (P, CTX)), ("nv", (P, CTX)), ("ns", (4, P, 2, 64)))


def program(nc, arrays):
    io = {k: nc.dram_tensor(f"in_{k}", a.shape, F32, kind="ExternalInput").ap() for k, a in arrays.items()}
    io["outs"] = [nc.dram_tensor(f"out_{k}", s, F32, kind="ExternalOutput").ap() for k, s in OUTS]
    build(nc, io)


def kernel(**inputs):
    import concourse.bacc as bacc
    from concourse.bass_utils import run_bass_kernel_spmd

    arrays = lay_out(inputs)
    nc = bacc.Bacc("TRN2", target_bir_lowering=False, num_devices=1)
    program(nc, arrays)
    r = run_bass_kernel_spmd(nc, [{f"in_{k}": a for k, a in arrays.items()}], core_ids=[0])
    y, nk, nv, ns = (r.results[0][f"out_{k}"] for k, _ in OUTS)
    y = y.transpose(2, 0, 1).reshape(TP, D)
    heads = lambda a: a.reshape(2, 64, CTX).transpose(0, 2, 1)[None, None]
    state = ns.reshape(4, 2, 64, 2, 64).transpose(3, 0, 1, 4, 2).reshape(1, 1, 2, 8, 64, 64)
    return (np.ascontiguousarray(y[None, C0:C0 + CTX]), np.ascontiguousarray(y[None, L0:L0 + LAT]),
            np.ascontiguousarray(heads(nk)), np.ascontiguousarray(heads(nv)), np.ascontiguousarray(state))
```
